# Optimizing a Trainium2 kernel written in Bass

```python
import jax, jax.numpy as jnp
from jax import lax
import numpy as np

D_MODEL = 1024
BATCH = 1
SEQ = 1024
DEPTH = 1
DEC_BATCH = 1
DEC_SEQ = 32
PAST_LEN = 128

CHUNK = 64
DSA_HEADS = 8
FOX_HEADS = 8
HEAD_DIM = D_MODEL // (DSA_HEADS + FOX_HEADS)
MIX_WIDTH = (DSA_HEADS + FOX_HEADS) * HEAD_DIM
DSA_KV_HEADS = 2
IDX_HEADS = 4
IDX_DIM = 64
TOPK_MAX = 256
ROPE_THETA = 500000.0
ROT_DIM = HEAD_DIM // 4
FORGET_BIAS_INIT = 2.0
N_MEM = 256
MEM_HEADS = 4
MEM_HEAD_DIM = D_MODEL // MEM_HEADS
PEER_HEADS = 8
PEER_KEY_DIM = 256
N_KEYS = 128
N_EXPERTS = N_KEYS * N_KEYS
PEER_TOPK = 16
Q_BLOCK = 128
TOK_BLOCK = 128
EPS = 1e-6
IN_SPLITS = (DSA_HEADS * HEAD_DIM, DSA_KV_HEADS * HEAD_DIM, DSA_KV_HEADS * HEAD_DIM, IDX_HEADS * IDX_DIM, IDX_DIM, IDX_HEADS, FOX_HEADS * HEAD_DIM, FOX_HEADS * HEAD_DIM, FOX_HEADS * HEAD_DIM, FOX_HEADS)
IN_WIDTH = int(sum(IN_SPLITS))
SPLIT_POINTS = tuple(int(c) for c in np.cumsum(IN_SPLITS)[:-1])

kernel_name = 'hybrid_dsa_fox_peer_stream_step'

def rms_norm(x, g):
    xf = x.astype(jnp.float32)
    y = xf * lax.rsqrt(jnp.mean(xf * xf, axis=-1, keepdims=True) + EPS)
    return (y * g.astype(jnp.float32)).astype(x.dtype)

def rope_partial(x, pos):
    inv_freq = ROPE_THETA ** (-jnp.arange(0, ROT_DIM, 2, dtype=jnp.float32) / ROT_DIM)
    ang = pos.astype(jnp.float32)[:, None] * inv_freq[None, :]
    ang = jnp.concatenate([ang, ang], axis=-1)
    shape = (1, pos.shape[0]) + (1,) * (x.ndim - 3) + (ROT_DIM,)
    cos = jnp.cos(ang).reshape(shape)
    sin = jnp.sin(ang).reshape(shape)
    xr = x[..., :ROT_DIM].astype(jnp.float32)
    x1, x2 = xr[..., :ROT_DIM // 2], xr[..., ROT_DIM // 2:]
    rot = jnp.concatenate([-x2, x1], axis=-1)
    xr = xr * cos + rot * sin
    return jnp.concatenate([xr.astype(x.dtype), x[..., ROT_DIM:]], axis=-1)

def sweep_queries(fn, q_tensors, q_pos):
    tq = q_pos.shape[0]
    if tq <= Q_BLOCK or tq % Q_BLOCK != 0:
        return fn(*q_tensors, q_pos)
    n = tq // Q_BLOCK
    blocks = tuple(jnp.moveaxis(t.reshape((t.shape[0], n, Q_BLOCK) + t.shape[2:]), 1, 0) for t in q_tensors)
    pos_b = q_pos.reshape(n, Q_BLOCK)
    out = lax.map(lambda a: fn(*a[0], a[1]), (blocks, pos_b))
    out = jnp.moveaxis(out, 0, 1)
    return out.reshape((out.shape[0], tq) + out.shape[3:])

def dsa_attention(q, qi, wi, k_all, v_all, ki_all, q_pos, k_pos, topk):
    def blk(q_b, qi_b, wi_b, pos_b):
        b, tb = q_b.shape[:2]
        idx = jax.nn.relu(jnp.einsum('bthd,bsd->bths', qi_b, ki_all))
        score = jnp.einsum('bths,bth->bts', idx, wi_b).astype(jnp.float32)
        admissible = (k_pos[None, :] // CHUNK) <= (pos_b[:, None] // CHUNK)
        score = jnp.where(admissible[None], score, -jnp.inf)
        sel_score, sel = lax.top_k(score, topk)
        valid = jnp.isfinite(sel_score)
        kg = jax.vmap(lambda kb, ib: kb[ib])(k_all, sel)
        vg = jax.vmap(lambda vb, ib: vb[ib])(v_all, sel)
        qg = q_b.reshape(b, tb, DSA_KV_HEADS, DSA_HEADS // DSA_KV_HEADS, HEAD_DIM)
        logits = jnp.einsum('btgrd,btkgd->btgrk', qg, kg).astype(jnp.float32) * (HEAD_DIM ** -0.5)
        logits = jnp.where(valid[:, :, None, None, :], logits, -jnp.inf)
        p = jax.nn.softmax(logits, axis=-1).astype(vg.dtype)
        o = jnp.einsum('btgrk,btkgd->btgrd', p, vg)
        return o.reshape(b, tb, DSA_HEADS * HEAD_DIM)
    return sweep_queries(blk, (q, qi, wi), q_pos)

def fox_attention(q, k_all, v_all, dq, dk_all, q_pos, k_pos):
    dk_t = jnp.swapaxes(dk_all, 1, 2)
    def blk(q_b, dq_b, pos_b):
        b, tb = q_b.shape[:2]
        logits = jnp.einsum('bthd,bshd->bhts', q_b, k_all).astype(jnp.float32) * (HEAD_DIM ** -0.5)
        logits = logits + jnp.swapaxes(dq_b, 1, 2)[:, :, :, None] - dk_t[:, :, None, :]
        mask = k_pos[None, :] <= pos_b[:, None]
        logits = jnp.where(mask[None, None], logits, -jnp.inf)
        p = jax.nn.softmax(logits, axis=-1).astype(v_all.dtype)
        o = jnp.einsum('bhts,bshd->bthd', p, v_all)
        return o.reshape(b, tb, FOX_HEADS * HEAD_DIM)
    return sweep_queries(blk, (q, dq), q_pos)

def memory_kv(mem, g, w_kv):
    b, m, _ = mem.shape
    kv = rms_norm(mem, g) @ w_kv
    k = kv[..., :D_MODEL].reshape(b, m, MEM_HEADS, MEM_HEAD_DIM)
    v = kv[..., D_MODEL:].reshape(b, m, MEM_HEADS, MEM_HEAD_DIM)
    return k, v

def memory_attention(xn, w_q, mk, mv, w_o):
    b, t, _ = xn.shape
    q = (xn @ w_q).reshape(b, t, MEM_HEADS, MEM_HEAD_DIM)
    logits = jnp.einsum('bthd,bmhd->bhtm', q, mk).astype(jnp.float32) * (MEM_HEAD_DIM ** -0.5)
    p = jax.nn.softmax(logits, axis=-1).astype(mv.dtype)
    o = jnp.einsum('bhtm,bmhd->bthd', p, mv).reshape(b, t, D_MODEL)
    return o @ w_o

def peer_ffn(xn, w_q, keys1, keys2, u, v):
    b, t, d = xn.shape
    n_tok = b * t
    pad = (-n_tok) % TOK_BLOCK
    tok = jnp.pad(xn.reshape(n_tok, d), ((0, pad), (0, 0)))
    blocks = tok.reshape(-1, TOK_BLOCK, d)
    half = PEER_KEY_DIM // 2
    def blk(xb):
        q = (xb @ w_q).reshape(TOK_BLOCK, PEER_HEADS, PEER_KEY_DIM)
        s1 = jnp.einsum('thd,hnd->thn', q[..., :half], keys1).astype(jnp.float32)
        s2 = jnp.einsum('thd,hnd->thn', q[..., half:], keys2).astype(jnp.float32)
        v1, i1 = lax.top_k(s1, PEER_TOPK)
        v2, i2 = lax.top_k(s2, PEER_TOPK)
        cand = (v1[..., :, None] + v2[..., None, :]).reshape(TOK_BLOCK, PEER_HEADS, PEER_TOPK * PEER_TOPK)
        cidx = (i1[..., :, None] * N_KEYS + i2[..., None, :]).reshape(TOK_BLOCK, PEER_HEADS, PEER_TOPK * PEER_TOPK)
        sv, si = lax.top_k(cand, PEER_TOPK)
        eidx = jnp.take_along_axis(cidx, si, axis=-1)
        g = jax.nn.softmax(sv, axis=-1)
        h = jax.nn.gelu(jnp.einsum('td,thkd->thk', xb, u[eidx]).astype(jnp.float32), approximate=False)
        return jnp.einsum('thk,thkd->td', (g * h).astype(v.dtype), v[eidx])
    out = lax.map(blk, blocks).reshape(-1, d)[:n_tok]
    return out.reshape(b, t, d)

def trunk_layer(x, pos, past, past_pos, mk, mv, norm_mix_g, w_in, b_fox_f, w_out, norm_mem_g, w_mem_q, w_mem_o, norm_ffn_g, peer_w_q, peer_keys1, peer_keys2, peer_u, peer_v):
    b, t, _ = x.shape
    xn = rms_norm(x, norm_mix_g)
    a_q, a_k, a_v, a_qi, a_ki, a_w, f_q, f_k, f_v, f_f = jnp.split(xn @ w_in, SPLIT_POINTS, axis=-1)
    a_q = rope_partial(a_q.reshape(b, t, DSA_HEADS, HEAD_DIM), pos)
    a_k = rope_partial(a_k.reshape(b, t, DSA_KV_HEADS, HEAD_DIM), pos)
    a_v = a_v.reshape(b, t, DSA_KV_HEADS, HEAD_DIM)
    a_qi = rope_partial(a_qi.reshape(b, t, IDX_HEADS, IDX_DIM), pos)
    a_ki = rope_partial(a_ki, pos)
    f_q = f_q.reshape(b, t, FOX_HEADS, HEAD_DIM)
    f_k = f_k.reshape(b, t, FOX_HEADS, HEAD_DIM)
    f_v = f_v.reshape(b, t, FOX_HEADS, HEAD_DIM)
    logf = jax.nn.log_sigmoid(f_f.astype(jnp.float32) + b_fox_f.astype(jnp.float32))
    new_rows = (a_k, a_v, a_ki, f_k, f_v, logf)
    if past is None:
        ak_all, av_all, aki_all, fk_all, fv_all, logf_all = new_rows
        k_pos = pos
    else:
        ak_all, av_all, aki_all, fk_all, fv_all, logf_all = tuple(jnp.concatenate([p, n], axis=1) for p, n in zip(past, new_rows))
        k_pos = jnp.concatenate([past_pos, pos], axis=0)
    n_keys_visible = ak_all.shape[1]
    topk = min(TOPK_MAX, n_keys_visible // 4)
    dk_all = jnp.cumsum(logf_all.astype(jnp.float32), axis=1)
    dq = dk_all[:, n_keys_visible - t:]
    o_a = dsa_attention(a_q, a_qi, a_w, ak_all, av_all, aki_all, pos, k_pos, topk)
    o_f = fox_attention(f_q, fk_all, fv_all, dq, dk_all, pos, k_pos)
    h = x + jnp.concatenate([o_a, o_f], axis=-1) @ w_out
    h = h + memory_attention(rms_norm(h, norm_mem_g), w_mem_q, mk, mv, w_mem_o)
    h = h + peer_ffn(rms_norm(h, norm_ffn_g), peer_w_q, peer_keys1, peer_keys2, peer_u, peer_v)
    return h, new_rows

def setup_inputs(seed: int = 0) -> dict:
    key = jax.random.key(seed)
    ks = jax.random.split(key, 32)
    f32 = jnp.float32
    def nrm(k, shape, scale):
        return jax.random.normal(k, shape, f32) * scale
    def gain(k, shape):
        return 1.0 + 0.05 * jax.random.normal(k, shape, f32)
    return {
        'x_prompt': nrm(ks[0], (BATCH, SEQ, D_MODEL), 1.0),
        'x_sample': nrm(ks[1], (DEC_BATCH, DEC_SEQ, D_MODEL), 1.0),
        'cache_dsa_k': nrm(ks[2], (DEPTH, DEC_BATCH, PAST_LEN, DSA_KV_HEADS, HEAD_DIM), 1.0),
        'cache_dsa_v': nrm(ks[3], (DEPTH, DEC_BATCH, PAST_LEN, DSA_KV_HEADS, HEAD_DIM), 1.0),
        'cache_dsa_kidx': nrm(ks[4], (DEPTH, DEC_BATCH, PAST_LEN, IDX_DIM), 1.0),
        'cache_fox_k': nrm(ks[5], (DEPTH, DEC_BATCH, PAST_LEN, FOX_HEADS, HEAD_DIM), 1.0),
        'cache_fox_v': nrm(ks[6], (DEPTH, DEC_BATCH, PAST_LEN, FOX_HEADS, HEAD_DIM), 1.0),
        'cache_fox_logf': jax.nn.log_sigmoid(FORGET_BIAS_INIT + jax.random.normal(ks[7], (DEPTH, DEC_BATCH, PAST_LEN, FOX_HEADS), f32)),
        'cache_mem_k': nrm(ks[8], (DEPTH, DEC_BATCH, N_MEM, MEM_HEADS, MEM_HEAD_DIM), 1.0),
        'cache_mem_v': nrm(ks[9], (DEPTH, DEC_BATCH, N_MEM, MEM_HEADS, MEM_HEAD_DIM), 1.0),
        'mem_prompt': nrm(ks[10], (BATCH, N_MEM, D_MODEL), 1.0),
        'norm_mix_g': gain(ks[11], (DEPTH, D_MODEL)),
        'w_in': nrm(ks[12], (DEPTH, D_MODEL, IN_WIDTH), D_MODEL ** -0.5),
        'b_fox_f': FORGET_BIAS_INIT + 0.5 * jax.random.normal(ks[13], (DEPTH, FOX_HEADS), f32),
        'w_out': nrm(ks[14], (DEPTH, MIX_WIDTH, D_MODEL), MIX_WIDTH ** -0.5),
        'mem_norm_g': gain(ks[15], (DEPTH, D_MODEL)),
        'w_mem_kv': nrm(ks[16], (DEPTH, D_MODEL, 2 * D_MODEL), D_MODEL ** -0.5),
        'norm_mem_g': gain(ks[17], (DEPTH, D_MODEL)),
        'w_mem_q': nrm(ks[18], (DEPTH, D_MODEL, D_MODEL), D_MODEL ** -0.5),
        'w_mem_o': nrm(ks[19], (DEPTH, D_MODEL, D_MODEL), D_MODEL ** -0.5),
        'norm_ffn_g': gain(ks[20], (DEPTH, D_MODEL)),
        'peer_w_q': nrm(ks[21], (DEPTH, D_MODEL, PEER_HEADS * PEER_KEY_DIM), D_MODEL ** -0.5),
        'peer_keys1': nrm(ks[22], (DEPTH, PEER_HEADS, N_KEYS, PEER_KEY_DIM // 2), (PEER_KEY_DIM // 2) ** -0.5),
        'peer_keys2': nrm(ks[23], (DEPTH, PEER_HEADS, N_KEYS, PEER_KEY_DIM // 2), (PEER_KEY_DIM // 2) ** -0.5),
        'peer_u': nrm(ks[24], (DEPTH, N_EXPERTS, D_MODEL), D_MODEL ** -0.5),
        'peer_v': nrm(ks[25], (DEPTH, N_EXPERTS, D_MODEL), 0.5),
        'final_norm_g': gain(ks[26], (D_MODEL,)),
    }

def reference(x_prompt, x_sample, cache_dsa_k, cache_dsa_v, cache_dsa_kidx, cache_fox_k, cache_fox_v, cache_fox_logf, cache_mem_k, cache_mem_v, mem_prompt, norm_mix_g, w_in, b_fox_f, w_out, mem_norm_g, w_mem_kv, norm_mem_g, w_mem_q, w_mem_o, norm_ffn_g, peer_w_q, peer_keys1, peer_keys2, peer_u, peer_v, final_norm_g):
    t_p = x_prompt.shape[1]
    t_s = x_sample.shape[1]
    past_len = cache_dsa_k.shape[2]
    pos_p = jnp.arange(t_p, dtype=jnp.int32)
    pos_past = jnp.arange(past_len, dtype=jnp.int32)
    pos_s = past_len + jnp.arange(t_s, dtype=jnp.int32)
    h_p, h_s = x_prompt, x_sample
    rows_p, rows_s = [], []
    for l in range(DEPTH):
        weights = (norm_mix_g[l], w_in[l], b_fox_f[l], w_out[l], norm_mem_g[l], w_mem_q[l], w_mem_o[l], norm_ffn_g[l], peer_w_q[l], peer_keys1[l], peer_keys2[l], peer_u[l], peer_v[l])
        mk_p, mv_p = memory_kv(mem_prompt, mem_norm_g[l], w_mem_kv[l])
        h_p, new_p = trunk_layer(h_p, pos_p, None, None, mk_p, mv_p, *weights)
        past = (cache_dsa_k[l], cache_dsa_v[l], cache_dsa_kidx[l], cache_fox_k[l], cache_fox_v[l], cache_fox_logf[l])
        h_s, new_s = trunk_layer(h_s, pos_s, past, pos_past, cache_mem_k[l], cache_mem_v[l], *weights)
        rows_p.append(new_p + (mk_p, mv_p))
        rows_s.append(new_s)
    y_prompt = rms_norm(h_p, final_norm_g)
    y_sample = rms_norm(h_s, final_norm_g)
    st_p = [jnp.stack([r[i] for r in rows_p], axis=0) for i in range(8)]
    st_s = [jnp.stack([r[i] for r in rows_s], axis=0) for i in range(6)]
    p_dsa_k, p_dsa_v, p_dsa_kidx, p_fox_k, p_fox_v, p_fox_logf, p_mem_k, p_mem_v = st_p
    s_dsa_k, s_dsa_v, s_dsa_kidx, s_fox_k, s_fox_v, s_fox_logf = st_s
    return (y_prompt, y_sample, p_dsa_k, p_dsa_v, p_dsa_kidx, p_fox_k, p_fox_v, p_fox_logf, p_mem_k, p_mem_v, s_dsa_k, s_dsa_v, s_dsa_kidx, s_fox_k, s_fox_v, s_fox_logf)


_drawn_inputs = setup_inputs


def setup_inputs(seed=0):
    import zlib

    import numpy as np

    out = dict(_drawn_inputs(seed))
    spreads = {}
    factors = {'norm_mem_g': 2.826}
    for name, (base, spread) in spreads.items():
        noise = np.random.default_rng([zlib.crc32(name.encode()), seed]).standard_normal(out[name].shape)
        drawn = base * np.exp(spread * noise) if base else spread * noise
        out[name] = __import__('jax').numpy.asarray(drawn.astype(out[name].dtype))
    for name, factor in factors.items():
        out[name] = (out[name] * factor).astype(out[name].dtype)
    return out
```

```python
from contextlib import ExitStack

import concourse.bass as bass
from concourse import mybir

F32 = mybir.dt.float32
BF16 = mybir.dt.bfloat16
U32 = mybir.dt.uint32
ACT = mybir.ActivationFunctionType
ALU = mybir.AluOpType
AX = mybir.AxisListType

P = 128
D = 1024
KD = D // P
T_P, T_S, PAST = 1024, 32, 128
NT = T_P + T_S
TG, NG = 352, 3
QT = 9
NK = T_P + PAST + T_S
HD = 64
VW = 640
EPS = 1e-6
NEG = -1e30
OUTSIDE = -1e38
TAKEN = -3e38
N_MEM, MH, MHD = 256, 4, 256
PH, NKEY, PK = 8, 128, 16
ROPE_THETA, ROT_DIM = 500000.0, 16

assert NT == TG * NG and NG * TG <= 1536

C_ID, C_CAUSAL, C_ROT, C_IOTA, C_SEL = 0, 128, 256, 384, 512
C_W = 520


def rows_of(t):
    return P if t < QT - 1 else T_S


def q_cols(t):
    return slice(t * P, t * P + rows_of(t))


def key_cols(t):
    return (0, P * (t + 1)) if t < QT - 1 else (T_P, PAST + T_S)


def key_blocks(t):
    return [(b, P) for b in range(t + 1)] if t < QT - 1 else [(8, P), (9, T_S)]


def groups_of(t):
    blocks = key_blocks(t)
    return [blocks[i:i + 4] for i in range(0, len(blocks), 4)]


SC_OFF = {t: sum(key_cols(s)[1] for s in range(2, t)) for t in range(2, QT)}
SC_W = sum(key_cols(s)[1] for s in range(2, QT))
MB_OFF = {t: sum(key_cols(s)[1] for s in range(t)) for t in range(QT)}
MB_W = sum(key_cols(s)[1] for s in range(QT))
UNITS = [(t, e) for t in range(QT) for e in range(2)]
NU = len(UNITS)
NGRP = sum(len(groups_of(t)) for t, e in UNITS)


NORMED = KD + 1


class Norm:

    def __init__(self, nc, sem, name, src, dst, gain, ones, sq, ps, root, w):
        self.nc, self.src, self.dst, self.gain, self.ones = nc, src, dst, gain, ones
        self.sq, self.ps, self.root, self.w = sq, ps, root, w
        self.spans = [(g, g * TG, min(w - g * TG, TG)) for g in range((w + TG - 1) // TG)]
        self.squared = sem(name + "_squared")
        self.summed = sem(name + "_summed")
        self.rooted = sem(name + "_rooted")
        self.normed = sem(name + "_normed")

    def act(self, act, eps):
        for k in range(KD):
            if k >= 2:
                act.wait_ge(self.summed, k - 1)
            act.activation(self.sq[:, k % 2, 0:self.w], self.src[:, k, 0:self.w],
                           ACT.Square).then_inc(self.squared, 1)
        act.wait_ge(self.summed, KD)
        for g, a, n in self.spans:
            act.activation(self.root[:, a:a + n], self.ps[:, g, 0:n], ACT.Sqrt,
                           scale=1.0 / D, bias=eps[:, 0:1]).then_inc(self.rooted, 1)

    def pe(self, pe):
        for k in range(KD):
            pe.wait_ge(self.squared, k + 1)
            for g, a, n in self.spans:
                mm = pe.matmul(self.ps[:, g, 0:n], self.ones, self.sq[:, k % 2, a:a + n],
                               start=(k == 0), stop=(k == KD - 1))
            mm.then_inc(self.summed, 1)

    def dve(self, dve):
        dve.wait_ge(self.rooted, len(self.spans))
        dve.reciprocal(self.root[:, 0:self.w], self.root[:, 0:self.w]).then_inc(self.normed, 1)
        dve.wait_ge(self.normed, 1)
        for k in range(KD):
            dve.scalar_tensor_tensor(out=self.dst[:, k, 0:self.w], in0=self.src[:, k, 0:self.w],
                                     scalar=self.gain[:, k:k + 1], in1=self.root[:, 0:self.w],
                                     op0=ALU.mult, op1=ALU.mult).then_inc(self.normed, 1)


class Project:

    def __init__(self, nc, sem, name, w_dram, M, wbuf, src, ps, w):
        self.w_dram, self.M, self.wbuf, self.src, self.ps = w_dram, M, wbuf, src, ps
        self.spans = [(g, g * TG, min(w - g * TG, TG)) for g in range((w + TG - 1) // TG)]
        self.w_ready = [sem(f"{name}_w{b}_ready") for b in range(2)]
        self.bank_ready = sem(name + "_bank_ready")
        self.bank_free = sem(name + "_bank_free")

    def sp(self, sp):
        n = len(self.spans)
        for b in range(2):
            sp.dma_start(self.wbuf[:, b], self.w_dram[b]).then_inc(self.w_ready[b], 16)
        with sp.Fori(1, self.M // 2) as i:
            for b in range(2):
                sp.wait_ge(self.bank_ready, (i * 2 + b - 1) * n)
                sp.dma_start(self.wbuf[:, b], self.w_dram[i * 2 + b]).then_inc(self.w_ready[b], 16)

    def pe(self, pe):
        n = len(self.spans)
        with pe.Fori(0, self.M // 2) as i:
            for b in range(2):
                pe.wait_ge(self.w_ready[b], (i + 1) * 16)
                for g, a, c in self.spans:
                    pe.wait_ge(self.bank_free, (i * 2 + b) * n + g + 1)
                    for k in range(KD):
                        mm = pe.matmul(self.ps[:, b * n + g, 0:c], self.wbuf[:, b, k, :],
                                       self.src[:, k, a:a + c], start=(k == 0), stop=(k == KD - 1))
                    mm.then_inc(self.bank_ready, 1)

    def out(self, eng, step):
        n = len(self.spans)
        eng.sem_inc(self.bank_free, 2 * n)
        with eng.Fori(0, self.M // 2) as i:
            for b in range(2):
                for g, a, c in self.spans:
                    eng.wait_ge(self.bank_ready, (i * 2 + b) * n + g + 1)
                    step(i * 2 + b, self.ps[:, b * n + g, 0:c], a, c).then_inc(self.bank_free, 1)

    def done(self, eng):
        eng.wait_ge(self.bank_free, (self.M + 2) * len(self.spans))


def mix_inputs(nc, sem, dram, keep):
    with ExitStack() as ctx:
        def sb(name, shape, dt=F32):
            return ctx.enter_context(nc.sbuf_tensor(name, shape, dt))

        con, ident, xn = keep["con"], keep["ident"], keep["xn"]
        xT = keep["oT"]
        eps = keep["eps"]
        cos, sin = keep["cs"][:, 0, :], keep["cs"][:, 1, :]
        rot = con[:, C_ROT:C_ROT + P]
        gain = sb("a_gain", [P, KD])
        ones = sb("a_ones", [P, P])
        sq = sb("a_sq", [P, 2, NT])
        root = sq[:, 0, :]
        raw = sq
        wv = sb("a_wv", [P, KD, VW + 4])
        wrope = sb("a_wrope", [P, 2, KD, P])
        wf = sb("a_wf", [P, KD, 8])
        qi = sb("a_qi", [P, 2, NT])
        kidx = sb("a_kidx", [P, NK])
        aw = sb("a_aw", [P, QT, 4])
        relu = sq[:, 0, 0:T_P]
        spare = keep["score"]
        tmp, tmp2 = spare[:, 2 * NT:2 * NT + TG], spare[:, 2 * NT + TG:2 * NT + 2 * TG]
        zz, za = spare[64:72, 0:NT], spare[64:72, NT:2 * NT]
        fb = sb("a_fb", [72, 1])[64:72, :]
        lf = keep["mbf"][64:72, 0:NK]
        ps = ctx.enter_context(nc.psum_tensor("a_ps", [P, 8, 512], F32))

        vnat, dk, gb, ka, score = keep["vnat"], keep["dk"], keep["gb"], keep["ka"], keep["score"]

        loaded = sem("a_loaded")
        w_rope = [sem(f"a_w_rope{b}") for b in range(2)]
        ones_set = sem("a_ones_set")
        norm = Norm(nc, sem, "a_norm", xT, xn, gain, ones[:, :], sq, ps, root, NT)
        raw_ready = sem("a_raw_ready")
        raw_copied = sem("a_raw_copied")
        rot_ready = sem("a_rot_ready")
        rot_sin = sem("a_rot_sin")
        rot_cos = sem("a_rot_cos")
        roped = sem("a_roped")
        f_ready = sem("a_f_ready")
        f_step = sem("a_f_step")
        f_act = sem("a_f_act")
        v_ready = sem("a_v_ready")
        v_copied = sem("a_v_copied")
        s_ready = sem("a_s_ready")
        s_relu = sem("a_s_relu")
        s_added = sem("a_s_added")
        stored = sem("a_stored")
        scanned = sem("a_scanned")

        def rope_dst(c, g):
            a = g * TG
            if c in (1, 2):
                return [(0, TG, qi[:, c - 1, a:a + TG])]
            d = ka if c == 0 else kidx
            if g < NG - 1:
                return [(0, TG, d[:, a:a + TG])]
            m = T_P - a
            return [(0, m, d[:, a:T_P]), (m, TG - m, d[:, T_P + PAST:NK])]

        NROPE = 4
        s_units = [(t, h) for t in range(2, QT) for h in range(4)]
        block = ctx.enter_context(nc.Block())

        @block.sync
        def _(sp):
            sp.dma_start(xT[:, :, :], dram["xT"]).then_inc(loaded, 16)
            sp.dma_start(con[:, :], dram["con"]).then_inc(loaded, 16)
            sp.dma_start(keep["cs"][:, :, :], dram["cs"]).then_inc(loaded, 16)
            sp.dma_start(gain[:, :], dram["g_mix"]).then_inc(loaded, 16)
            sp.dma_start(fb, dram["fb"]).then_inc(loaded, 16)
            for b in range(2):
                sp.dma_start(wrope[:, b], dram["w_rope"][b]).then_inc(w_rope[b], 16)
            sp.dma_start(wf[:, :, :], dram["w_f"]).then_inc(loaded, 16)
            sp.dma_start(wv[:, :, :], dram["w_v"]).then_inc(loaded, 16)
            sp.dma_start(ka[:, T_P:T_P + PAST], dram["c_ka"]).then_inc(loaded, 16)
            sp.dma_start(kidx[:, T_P:T_P + PAST], dram["c_kidx"]).then_inc(loaded, 16)
            sp.dma_start(lf[:, T_P:T_P + PAST], dram["c_logf"]).then_inc(loaded, 16)
            sp.dma_start(vnat[:, 8, :], dram["c_v"]).then_inc(loaded, 16)
            for b in range(2):
                sp.wait_ge(raw_ready, NG * (b + 1))
                sp.dma_start(wrope[:, b], dram["w_rope"][2 + b]).then_inc(w_rope[b], 16)
            for t in range(QT):
                sp.wait_ge(v_copied, 3 * (t + 1))
                M = rows_of(t)
                tile = t if t < 8 else 9
                sp.dma_start(dram["o_v"][t * P:t * P + M, :], vnat[0:M, tile, :]).then_inc(stored, 16)
            sp.wait_ge(roped, NG * NROPE)
            sp.dma_start(dram["o_ka"], ka[:, :]).then_inc(stored, 16)
            sp.dma_start(dram["o_kidx"], kidx[0:HD, :]).then_inc(stored, 16)
            sp.wait_ge(f_step, 5)
            sp.dma_start(dram["o_logf"], lf[:, :]).then_inc(stored, 16)
            sp.wait_ge(stored, 16 * (QT + 3))

        @block.tensor
        def _(pe):
            pe.wait_ge(loaded, 176)
            pe.wait_ge(ones_set, 1)
            norm.pe(pe)
            pe.wait_ge(norm.normed, NORMED)
            pe.wait_ge(norm.rooted, NG)

            def project(c):
                pe.wait_ge(w_rope[c % 2], 16 * (c // 2 + 1))
                if c >= 2:
                    pe.wait_ge(raw_copied, NG * (c - 1))
                for g in range(NG):
                    for k in range(KD):
                        mm = pe.matmul(ps[:, 3 * (c % 2) + g, 0:TG], wrope[:, c % 2, k, :],
                                       xn[:, k, g * TG:(g + 1) * TG], start=(k == 0), stop=(k == KD - 1))
                    mm.then_inc(raw_ready, 1)

            def rotate(c):
                for g in range(NG):
                    n = NG * c + g
                    pe.wait_ge(raw_copied, n + 1)
                    if n >= 2:
                        pe.wait_ge(rot_sin, n - 1)
                    pe.matmul(ps[:, 6 + n % 2, 0:TG], rot, raw[:, c % 2, g * TG:(g + 1) * TG],
                              start=True, stop=True).then_inc(rot_ready, 1)

            project(0)
            for c in range(1, NROPE):
                project(c)
                rotate(c - 1)
            pe.wait_ge(raw_copied, NG * 3)
            for g in range(NG):
                for k in range(KD):
                    mm = pe.matmul(ps[0:8, g, 0:TG], wf[:, k, :], xn[:, k, g * TG:(g + 1) * TG],
                                   start=(k == 0), stop=(k == KD - 1))
                mm.then_inc(f_ready, 1)
            rotate(NROPE - 1)
            for t in range(QT):
                M, b = rows_of(t), 2 * (t % 2)
                if t < 2:
                    pe.wait_ge(f_step, 1)
                    pe.wait_ge(raw_copied, NG * NROPE)
                else:
                    pe.wait_ge(v_copied, 3 * (t - 1))
                for a, n, bank in ((0, 512, b), (512, VW + 4 - 512, b + 1)):
                    for k in range(KD):
                        mm = pe.matmul(ps[0:M, bank, 0:n], xn[:, k, q_cols(t)], wv[:, k, a:a + n],
                                       start=(k == 0), stop=(k == KD - 1))
                mm.then_inc(v_ready, 1)
            pe.wait_ge(roped, NG * NROPE)
            for u, (t, h) in enumerate(s_units):
                M, b, r = rows_of(t), 4 + 2 * (u % 2), HD * (h % 2)
                if u < 2:
                    pe.wait_ge(rot_sin, NG * NROPE)
                else:
                    pe.wait_ge(s_relu, u - 1)
                first, count = key_cols(t)
                for a in range(0, count, 512):
                    n = min(512, count - a)
                    mm = pe.matmul(ps[0:M, b + a // 512, 0:n], qi[r:r + HD, h // 2, q_cols(t)],
                                   kidx[r:r + HD, first + a:first + a + n], start=True, stop=True)
                mm.then_inc(s_ready, 1)

        @block.scalar
        def _(act):
            act.wait_ge(loaded, 176)
            act.wait_ge(ones_set, 2)
            norm.act(act, eps)
            for c in range(NROPE):
                for g in range(NG):
                    act.wait_ge(raw_ready, NG * c + g + 1)
                    if c < 2:
                        act.wait_ge(norm.normed, NORMED)
                    if c >= 2:
                        act.wait_ge(roped, NG * (c - 2) + g + 1)
                    act.activation(raw[:, c % 2, g * TG:(g + 1) * TG], ps[:, 3 * (c % 2) + g, 0:TG],
                                   ACT.Copy).then_inc(raw_copied, 1)
            act.wait_ge(f_step, 3)
            act.activation(zz[:, :], zz[:, :], ACT.Exp, scale=-1.0).then_inc(f_act, 1)
            act.wait_ge(f_act, 1)
            act.activation(zz[:, :], zz[:, :], ACT.Ln, bias=1.0).then_inc(f_act, 1)
            act.wait_ge(ones_set, 9)
            for t in range(QT):
                act.wait_ge(v_ready, t + 1)
                M, b, tile = rows_of(t), 2 * (t % 2), t if t < 8 else 9
                act.activation(vnat[0:M, tile, 0:512], ps[0:M, b, 0:512], ACT.Copy).then_inc(v_copied, 1)
                act.activation(vnat[0:M, tile, 512:VW], ps[0:M, b + 1, 0:VW - 512],
                               ACT.Copy).then_inc(v_copied, 1)
                act.activation(aw[0:M, t, :], ps[0:M, b + 1, VW - 512:VW - 508], ACT.Copy).then_inc(v_copied, 1)
            for u, (t, h) in enumerate(s_units):
                M, b = rows_of(t), 4 + 2 * (u % 2)
                count = key_cols(t)[1]
                act.wait_ge(s_ready, u + 1)
                if u >= 1:
                    act.wait_ge(s_added, u)
                src = ps[0:M, b:b + 2, :].rearrange("p a b -> p (a b)")[:, 0:count]
                act.activation(relu[0:M, 0:count], src, ACT.Relu).then_inc(s_relu, 1)

        @block.vector
        def _(dve):
            dve.memset(ones[:, :], 1.0).then_inc(ones_set, 1)
            dve.memset(eps[:, :], EPS).then_inc(ones_set, 1)
            dve.memset(dk[64:104, :], 0.0).then_inc(ones_set, 1)
            dve.memset(gb[64:104, :], 0.0).then_inc(ones_set, 1)
            dve.wait_ge(ones_set, 4)
            dve.memset(dk[96:104, :], 1.0).then_inc(ones_set, 1)
            dve.memset(gb[64:72, :], 1.0).then_inc(ones_set, 1)
            dve.memset(vnat[:, 9, :], 0.0).then_inc(ones_set, 1)
            dve.wait_ge(loaded, 176)
            dve.tensor_copy(keep["causal"][:, :], con[:, C_CAUSAL:C_CAUSAL + P]).then_inc(ones_set, 1)
            dve.tensor_copy(keep["identb"][:, :], ident).then_inc(ones_set, 1)
            norm.dve(dve)

            def combine(c):
                for g in range(NG):
                    n = NG * c + g
                    cols = slice(g * TG, (g + 1) * TG)
                    dve.wait_ge(rot_ready, n + 1)
                    if n >= 1:
                        dve.wait_ge(roped, n)
                    dve.tensor_tensor(tmp[:, :], ps[:, 6 + n % 2, 0:TG], sin[:, cols],
                                      ALU.mult).then_inc(rot_sin, 1)
                    dve.tensor_tensor(tmp2[:, :], raw[:, c % 2, cols], cos[:, cols],
                                      ALU.mult).then_inc(rot_cos, 1)
                    dve.wait_ge(rot_sin, n + 1)
                    dve.wait_ge(rot_cos, n + 1)
                    for a, m, d in rope_dst(c, g):
                        op = dve.tensor_tensor(d, tmp[:, a:a + m], tmp2[:, a:a + m], ALU.add)
                    op.then_inc(roped, 1)

            for c in range(NROPE - 1):
                combine(c)
            dve.wait_ge(f_ready, NG)
            for g in range(NG):
                op = dve.tensor_scalar(za[:, g * TG:(g + 1) * TG], ps[0:8, g, 0:TG], fb[:, 0:1], None, ALU.add)
            op.then_inc(f_step, 1)
            dve.wait_ge(f_step, 1)
            dve.tensor_scalar(zz[:, :], za[:, :], -1.0, None, ALU.mult).then_inc(f_step, 1)
            dve.wait_ge(f_step, 2)
            dve.tensor_tensor(zz[:, :], zz[:, :], za[:, :], ALU.max).then_inc(f_step, 1)
            combine(NROPE - 1)
            dve.wait_ge(f_act, 2)
            dve.scalar_tensor_tensor(out=lf[:, 0:T_P], in0=za[:, 0:T_P], scalar=0.0, in1=zz[:, 0:T_P],
                                     op0=ALU.min, op1=ALU.subtract).then_inc(f_step, 1)
            dve.scalar_tensor_tensor(out=lf[:, T_P + PAST:NK], in0=za[:, T_P:NT], scalar=0.0,
                                     in1=zz[:, T_P:NT], op0=ALU.min, op1=ALU.subtract).then_inc(f_step, 1)
            dve.wait_ge(f_step, 5)
            dve.wait_ge(ones_set, 9)
            for a, b in ((0, T_P), (T_P, NK)):
                dve.tensor_tensor_scan(dk[64:72, a:b], gb[64:72, a:b], lf[:, a:b], 0.0,
                                       ALU.mult, ALU.add).then_inc(scanned, 1)
            dve.wait_ge(scanned, 2)
            dve.tensor_scalar(gb[96:104, :], dk[64:72, :], -1.0, None, ALU.mult).then_inc(scanned, 1)
            dve.wait_ge(v_copied, 3 * QT)
            for u, (t, h) in enumerate(s_units):
                M, count = rows_of(t), key_cols(t)[1]
                dve.wait_ge(s_relu, u + 1)
                dst = score[0:M, SC_OFF[t]:SC_OFF[t] + count]
                if h == 0:
                    op = dve.tensor_scalar(dst, relu[0:M, 0:count], aw[0:M, t, 0:1], None, ALU.mult)
                else:
                    dve.wait_ge(s_added, u)
                    op = dve.scalar_tensor_tensor(out=dst, in0=relu[0:M, 0:count], scalar=aw[0:M, t, h:h + 1],
                                                  in1=dst, op0=ALU.mult, op1=ALU.add)
                op.then_inc(s_added, 1)
            dve.wait_ge(s_added, len(s_units))
            for t in range(2, QT - 1):
                dve.memset(score[0:HD, SC_OFF[t] + P * t + HD:SC_OFF[t] + P * (t + 1)], OUTSIDE)


def attention_pairs(nc, sem, dram, keep, fox):
    tag = "f" if fox else "d"
    with ExitStack() as ctx:
        def sb(name, shape, dt=F32):
            return ctx.enter_context(nc.sbuf_tensor(f"{tag}_{name}", shape, dt))

        def S(name):
            return sem(f"{tag}_{name}")

        con, ident, xn, oT = keep["con"], keep["ident"], keep["xn"], keep["oT"]
        vnat, dk, gb, score, mb = keep["vnat"], keep["dk"], keep["gb"], keep["score"], keep["mb"]
        cos, sin = keep["cs"][:, 0, :], keep["cs"][:, 1, :]
        w = sb("w", [P, 2 if fox else 1, KD, P])
        q = sb("q", [P, 2, NT]) if fox else sb("q", [P, NT])
        k = sb("k", [P, 2, NK]) if fox else keep["ka"]
        raw = None if fox else sb("raw", [P, NT])
        tmp = None if fox else sb("tmp", [P, TG])
        tmp2 = None if fox else sb("tmp2", [P, TG])
        pr = sb("p", [P, 2, T_P])
        pt = sb("pt", [P, 2, 8, P])
        opair = sb("opair", [P, 2, P])
        nmax = sb("nmax", [P, 2])
        rsum = sb("rsum", [P, 2])
        rinv = sb("rinv", [P, 2])
        best = sb("best", [P, QT, 8]) if fox else None
        s_ps = ctx.enter_context(nc.psum_tensor(f"{tag}_s_ps", [P, 4, 512], F32))
        t_ps = ctx.enter_context(nc.psum_tensor(f"{tag}_t_ps", [P, 2, 4, P], F32))
        o_ps = ctx.enter_context(nc.psum_tensor(f"{tag}_o_ps", [P, 2, 512], F32))
        x_ps = o_ps[:, 1, P:2 * P]

        NP_ = 6
        w_ready = S("w_ready")
        p_ready, p_copied = S("proj_ready"), S("proj_copied")
        if fox:
            bh_ready, store = S("bias_rows_ready"), S("k_stored")
            picked, dropped, masked = S("picked"), S("dropped"), S("masked")
        else:
            roped, rsin, rcos = S("roped"), S("rot_sin"), S("rot_cos")
        qk_ready, max_ready, p_exp = S("qk_ready"), S("max_ready"), S("exp_done")
        pt_ready, pt_copied = S("pt_ready"), S("pt_copied")
        pv_ready, o_inv, o_normed = S("pv_ready"), S("o_inv"), S("o_normed")
        x_ready, x_copied = S("x_ready"), S("x_copied")
        passed = S("passed")
        n_w = 4 if fox else 1
        copies = 6 if fox else 3

        block = ctx.enter_context(nc.Block())

        @block.sync
        def _(sp):
            with sp.Fori(0, 4) as j:
                sp.wait_ge(p_ready, j * NP_ + 1)
                if fox:
                    sp.wait_ge(qk_ready, j * NU + 1)
                    sp.dma_start(w[:, 0], dram["w_fq"][j]).then_inc(w_ready, 16)
                    sp.dma_start(w[:, 1], dram["w_fk"][j]).then_inc(w_ready, 16)
                    for e in range(2):
                        sp.dma_start(k[0:HD, e, T_P:T_P + PAST], dram["c_fk"][j * 2 + e]).then_inc(w_ready, 16)
                    sp.wait_ge(p_copied, j * copies + copies)
                    for e in range(2):
                        sp.dma_start(dram["o_fk"][j * 2 + e], k[0:HD, e, :]).then_inc(store, 16)
                else:
                    sp.dma_start(w[:, 0], dram["w_aq"][j]).then_inc(w_ready, 16)
            if fox:
                sp.wait_ge(store, 32 * 4 + 16)

        @block.tensor
        def _(pe):
            pe.sem_inc(p_ready, 1)
            pe.sem_inc(qk_ready, 1)
            pe.sem_inc(x_ready, 2)

            def project(j, r, wi, g):
                for kk in range(KD):
                    mm = pe.matmul(s_ps[:, r % 4, 0:TG], w[:, wi, kk, :], xn[:, kk, g * TG:(g + 1) * TG],
                                   start=(kk == 0), stop=(kk == KD - 1))
                mm.then_inc(p_ready, 1)

            def scores(j, u):
                t, e = UNITS[u]
                M, r = rows_of(t), HD * e
                first, count = key_cols(t)
                pe.wait_ge(p_exp, j * NU + u + 1)
                settled(t)
                for a in range(0, count, 512):
                    n = min(512, count - a)
                    dst = s_ps[0:M, 2 * (u % 2) + a // 512, 0:n]
                    last = a + n == count
                    if fox:
                        mm = pe.matmul(dst, q[0:104, e, q_cols(t)], k[0:104, e, first + a:first + a + n],
                                       start=True, stop=not last)
                        if last:
                            m = min(P, M)
                            mm = pe.matmul(dst[:, n - m:n], keep["identb"][0:M, 0:M], keep["causal"][0:M, 0:m],
                                           start=False, stop=True)
                    else:
                        pe.matmul(dst, q[r:r + HD, q_cols(t)], k[r:r + HD, first + a:first + a + n],
                                  start=True, stop=False)
                        mm = pe.matmul(dst, keep["identb"][0:M, 0:M],
                                       mb[0:M, MB_OFF[t] + a:MB_OFF[t] + a + n], start=False, stop=True)
                mm.then_inc(qk_ready, 1)

            def settled(t):
                if t == QT - 1:
                    pe.sem_inc(passed, 1)

            def head_out(j, t):
                M = rows_of(t)
                pe.wait_ge(o_normed, j * NU + 2 * t + 4)
                pe.wait_ge(x_copied, j * QT + t + 1)
                settled(t)
                pe.transpose(x_ps[:, 0:M], opair[0:M, t % 2, :], ident[0:M, 0:M]).then_inc(x_ready, 1)

            with pe.Fori(0, 4) as j:
                pe.wait_ge(w_ready, (j + 1) * (16 * n_w))
                pe.wait_ge(p_exp, j * NU + 2)
                if fox:
                    for r in range(6):
                        if r >= 4:
                            pe.wait_ge(p_copied, j * copies + r - 3)
                        project(j, r, r // 3, r % 3)
                    pe.wait_ge(p_copied, (j + 1) * copies)
                    pe.wait_ge(bh_ready, j * 2 + 4)
                else:
                    for g in range(NG):
                        project(j, g, 0, g)
                    for g in range(NG):
                        pe.wait_ge(p_copied, j * copies + g + 1)
                        if g == 2:
                            pe.wait_ge(p_copied, j * copies + 2)
                        bank = (3, 0, 1)[g]
                        pe.matmul(s_ps[:, bank, 0:TG], con[:, C_ROT:C_ROT + P], raw[:, g * TG:(g + 1) * TG],
                                  start=True, stop=True).then_inc(p_ready, 1)
                    pe.wait_ge(roped, (j + 1) * NG)
                scores(j, 0)
                group = 0
                for u, (t, e) in enumerate(UNITS):
                    M = rows_of(t)
                    if u + 1 < NU:
                        scores(j, u + 1)
                    pe.wait_ge(p_exp, j * NU + u + 3)
                    n = 0
                    for blocks in groups_of(t):
                        pe.wait_ge(pt_copied, j * NGRP + group + 1)
                        settled(t)
                        for i, (b, kw) in enumerate(blocks):
                            mm = pe.transpose(t_ps[0:kw, group % 2, i, 0:M],
                                              pr[0:M, u % 2, P * n:P * n + kw], ident[0:M, 0:M])
                            n += 1
                        mm.then_inc(pt_ready, 1)
                        group += 1
                    pe.wait_ge(o_normed, j * NU + u + 1)
                    if e == 1:
                        pe.wait_ge(x_copied, j * QT + t + 1)
                    nb = len(key_blocks(t))
                    pe.wait_ge(pt_copied, j * NGRP + group + 2)
                    for i, (b, _) in enumerate(key_blocks(t)):
                        vc = (j * 2 + e) * HD if fox else 512 + e * HD
                        mm = pe.matmul(o_ps[0:M, u % 2, 0:HD], pt[:, u % 2, i, 0:M],
                                       vnat[:, b, bass.ds(vc, HD)], start=(i == 0), stop=(i == nb - 1))
                    mm.then_inc(pv_ready, 1)
                    if e == 0 and t >= 1:
                        head_out(j, t - 1)
                head_out(j, QT - 1)

        def tile_out(act, j, t):
            M = rows_of(t)
            act.wait_ge(x_ready, j * QT + t + 3)
            act.activation(oT[:, j + (4 if fox else 0), q_cols(t)], x_ps[:, 0:M], ACT.Copy).then_inc(x_copied, 1)

        @block.scalar
        def _(act):
            act.sem_inc(p_exp, 2)
            act.sem_inc(pt_copied, 2)
            with act.Fori(0, 4) as j:
                if fox:
                    act.wait_ge(store, j * 32 + 16)
                    for r in range(6):
                        act.wait_ge(p_ready, j * NP_ + r + 2)
                        g = r % 3
                        src = s_ps[:, r % 4, 0:TG]
                        for e in range(2):
                            half = src[e * HD:(e + 1) * HD]
                            if r < 3:
                                op = act.activation(q[0:HD, e, g * TG:(g + 1) * TG], half, ACT.Copy, scale=HD ** -0.5)
                            elif g < 2:
                                op = act.activation(k[0:HD, e, g * TG:(g + 1) * TG], half, ACT.Copy)
                            else:
                                m = T_P - g * TG
                                act.activation(k[0:HD, e, g * TG:T_P], half[:, 0:m], ACT.Copy)
                                op = act.activation(k[0:HD, e, T_P + PAST:NK], half[:, m:TG], ACT.Copy)
                        op.then_inc(p_copied, 1)
                else:
                    for g in range(NG):
                        act.wait_ge(p_ready, j * NP_ + g + 2)
                        act.activation(raw[:, g * TG:(g + 1) * TG], s_ps[:, g, 0:TG], ACT.Copy,
                                       scale=HD ** -0.5).then_inc(p_copied, 1)
                group = 0
                for u, (t, e) in enumerate(UNITS):
                    M, count = rows_of(t), key_cols(t)[1]
                    src = s_ps[0:M, 2 * (u % 2):2 * (u % 2) + 2, :].rearrange("p a b -> p (a b)")[:, 0:count]
                    act.wait_ge(max_ready, j * NU + u + 1)
                    act.wait_ge(pv_ready, j * NU + u + 1)
                    act.wait_ge(o_inv, j * NU + u + 1)
                    act.activation(pr[0:M, u % 2, 0:count], src, ACT.Exp, bias=nmax[0:M, u % 2:u % 2 + 1],
                                   accum_out=rsum[0:M, u % 2:u % 2 + 1]).then_inc(p_exp, 1)
                    n = 0
                    for blocks in groups_of(t):
                        act.wait_ge(pt_ready, j * NGRP + group + 1)
                        m = len(blocks)
                        if t < QT - 1:
                            act.activation(pt[:, u % 2, n:n + m, :], t_ps[:, group % 2, 0:m, :],
                                           ACT.Copy).then_inc(pt_copied, 1)
                        else:
                            act.activation(pt[:, u % 2, 0, 0:M], t_ps[:, group % 2, 0, 0:M], ACT.Copy)
                            act.activation(pt[0:M, u % 2, 1, 0:M], t_ps[0:M, group % 2, 1, 0:M],
                                           ACT.Copy).then_inc(pt_copied, 1)
                        n += m
                        group += 1
                    if e == 0 and t >= 1:
                        tile_out(act, j, t - 1)
                tile_out(act, j, QT - 1)

        @block.vector
        def _(dve):
            dve.sem_inc(o_normed, 2)
            dve.sem_inc(x_copied, 1)
            dve.sem_inc(pv_ready, 2)
            dve.sem_inc(o_inv, 2)
            if fox:
                dve.sem_inc(store, 16)
                dve.sem_inc(dropped, 6)
                for e in range(2):
                    dve.tensor_copy(q[64:104, e, 0:T_P], dk[64:104, 0:T_P])
                    dve.tensor_copy(q[64:104, e, T_P:NT], dk[64:104, T_P + PAST:NK]).then_inc(bh_ready, 1)
                turns = [t for r in range(8) for t in range(2, QT - 1)]
                NR = len(turns)
                share = [turns[NR * u // NU:NR * (u + 1) // NU] for u in range(NU)]
            with dve.Fori(0, 4) as j:
                if fox:
                    for e in range(2):
                        dve.wait_ge(pv_ready, j * NU + 2)
                        dve.tensor_scalar(k[64:104, e, :], gb[64:104, :],
                                          con[64:104, bass.ds(j * 2 + (C_SEL + e), 1)],
                                          None, ALU.mult).then_inc(bh_ready, 1)
                else:
                    for g in range(NG):
                        cols = slice(g * TG, (g + 1) * TG)
                        bank = (3, 0, 1)[g]
                        dve.wait_ge(p_ready, j * NP_ + g + 5)
                        dve.tensor_tensor(tmp[:, :], s_ps[:, bank, 0:TG], sin[:, cols], ALU.mult).then_inc(rsin, 1)
                        dve.tensor_tensor(tmp2[:, :], raw[:, cols], cos[:, cols], ALU.mult).then_inc(rcos, 1)
                        dve.wait_ge(rsin, j * NG + g + 1)
                        dve.wait_ge(rcos, j * NG + g + 1)
                        dve.tensor_tensor(q[:, cols], tmp[:, :], tmp2[:, :], ALU.add).then_inc(roped, 1)
                        dve.wait_ge(roped, j * NG + g + 1)

                def row_max(u):
                    t, e = UNITS[u]
                    M, count = rows_of(t), key_cols(t)[1]
                    src = s_ps[0:M, 2 * (u % 2):2 * (u % 2) + 2, :].rearrange("p a b -> p (a b)")[:, 0:count]
                    dve.wait_ge(qk_ready, j * NU + u + 2)
                    dve.wait_ge(p_exp, j * NU + u + 1)
                    dve.tensor_reduce(nmax[0:M, u % 2:u % 2 + 1], src, AX.X, ALU.max,
                                      negate=True).then_inc(max_ready, 1)

                row_max(0)
                n_turn = 0
                for u, (t, e) in enumerate(UNITS):
                    M = rows_of(t)
                    if u + 1 < NU:
                        row_max(u + 1)
                    if fox:
                        for tt in share[u]:
                            n = key_cols(tt)[1]
                            s = score[:, SC_OFF[tt]:SC_OFF[tt] + n]
                            dve.wait_ge(dropped, j * NR + n_turn + 1)
                            dve.sem_inc(passed, 1)
                            dve.max(best[:, tt, :], s).then_inc(picked, 1)
                            n_turn += 1
                            dve.wait_ge(picked, j * NR + n_turn)
                            dve.sem_inc(passed, 1)
                            dve.match_replace(s, best[:, tt, :], s, TAKEN).then_inc(dropped, 1)
                    dve.wait_ge(p_exp, j * NU + u + 3)
                    dve.reciprocal(rinv[0:M, u % 2:u % 2 + 1], rsum[0:M, u % 2:u % 2 + 1]).then_inc(o_inv, 1)
                    dve.wait_ge(o_inv, j * NU + u + 3)
                    dve.wait_ge(pv_ready, j * NU + u + 3)
                    if e == 0:
                        dve.wait_ge(x_ready, j * QT + max(t + 1, 2))
                    dve.tensor_scalar(opair[0:M, t % 2, e * HD:(e + 1) * HD], o_ps[0:M, u % 2, 0:HD],
                                      rinv[0:M, u % 2:u % 2 + 1], None, ALU.mult).then_inc(o_normed, 1)

            if fox:
                dve.wait_ge(dropped, 4 * NR + 6)
                for r in range(5):
                    s = score[0:T_S, SC_OFF[8]:SC_OFF[8] + PAST + T_S]
                    dve.max(best[0:T_S, 8, :], s).then_inc(picked, 1)
                    dve.wait_ge(picked, 4 * NR + r + 1)
                    dve.match_replace(s, best[0:T_S, 8, :], s, TAKEN).then_inc(dropped, 1)
                    dve.wait_ge(dropped, 4 * NR + r + 7)
                dve.memset(mb[:, 0:MB_OFF[2]], 0.0).then_inc(masked, 1)
                dve.wait_ge(masked, 1)
                for t in range(2):
                    dve.memset(mb[0:HD, MB_OFF[t] + P * t + HD:MB_OFF[t] + P * (t + 1)], NEG)
                for t in range(2, QT):
                    M, n = rows_of(t), key_cols(t)[1]
                    dve.tensor_scalar(mb[0:M, MB_OFF[t]:MB_OFF[t] + n], score[0:M, SC_OFF[t]:SC_OFF[t] + n],
                                      -2e38, NEG, ALU.is_gt, ALU.mult)


def memory_and_mixer(nc, sem, dram, keep):
    with ExitStack() as ctx:
        def sb(name, shape, dt=F32):
            return ctx.enter_context(nc.sbuf_tensor(f"m_{name}", shape, dt))

        con, ident, oT, h, pq, eps = (keep[n] for n in ("con", "ident", "oT", "h", "pq", "eps"))
        ones = sb("ones", [P, P])
        gains = sb("gains", [P, 3, KD])
        wbuf = sb("w", [P, 2, KD, P])
        sq = sb("sq", [P, 2, NT])
        root = sq[:, 0, :]
        mkT = sb("mkT", [P, 2, KD, N_MEM])
        mv = sb("mv", [P, 2, 2, D])
        flat = pq[:, 8:16, :].rearrange("p a b -> p (a b)")
        wmv = flat[:, 0:KD * D].rearrange("p (k n) -> p k n", k=KD)
        memT = pq[:, 0:2, :].rearrange("p a b -> p (a b)")[:, 0:KD * N_MEM].rearrange("p (k n) -> p k n", k=KD)
        pr = sb("p", [P, 2, N_MEM])
        prn = sb("pn", [P, 2, N_MEM])
        pt = sb("pt", [P, 2, 2, P])
        nmax, rsum, rinv = sb("nmax", [P, 2]), sb("rsum", [P, 2]), sb("rinv", [P, 2])
        ps = ctx.enter_context(nc.psum_tensor("m_ps", [P, 8, 512], F32))

        loaded, set_ = sem("m_loaded"), sem("m_set")
        mem_loaded = sem("m_mem_loaded")
        stored = sem("m_stored")
        v_ready, v_copied = sem("m_v_ready"), sem("m_v_copied")
        out_proj = Project(nc, sem, "m_out", dram["w_out"], 8, wbuf, oT, ps, NT)
        norm_m = Norm(nc, sem, "m_nm", memT, memT, gains[:, 0], ones[:, :], sq, ps[:, 6:8], root, N_MEM)
        k_proj = Project(nc, sem, "m_k", dram["w_mk"], 8, wbuf, memT, ps, N_MEM)
        norm_q = Norm(nc, sem, "m_nq", h, oT, gains[:, 1], ones[:, :], sq, ps, root, NT)
        q_proj = Project(nc, sem, "m_q", dram["w_mq"], 8, wbuf, oT, ps, NT)
        o_proj = Project(nc, sem, "m_o", dram["w_mo"], 8, wbuf, oT, ps, NT)
        norm_f = Norm(nc, sem, "m_nf", h, oT, gains[:, 2], ones[:, :], sq, ps, root, NT)
        f_proj = Project(nc, sem, "m_f", dram["w_pq"], 16, wbuf, oT, ps, NT)
        units = [(t, m) for t in range(QT) for m in range(MH)]
        s_ready, s_max, s_exp, s_inv, s_norm = (sem("m_" + n) for n in
                                                ("s_ready", "s_max", "s_exp", "s_inv", "s_norm"))
        t_ready, t_copied, a_ready, a_copied = (sem("m_" + n) for n in
                                                ("t_ready", "t_copied", "a_ready", "a_copied"))

        block = ctx.enter_context(nc.Block())

        @block.sync
        def _(sp):
            sp.dma_start(h[:, :, :], dram["xT"]).then_inc(loaded, 16)
            sp.dma_start(gains[:, :, :], dram["g_rest"]).then_inc(loaded, 16)
            out_proj.sp(sp)
            sp.dma_start(memT, dram["memT"]).then_inc(mem_loaded, 16)
            sp.dma_start(wmv, dram["w_mv"]).then_inc(mem_loaded, 16)
            sp.dma_start(mkT[:, 1], dram["c_mk"]).then_inc(mem_loaded, 16)
            sp.dma_start(mv[:, 1], dram["c_mv"]).then_inc(mem_loaded, 16)
            sp.wait_ge(out_proj.bank_ready, 8 * NG)
            k_proj.sp(sp)
            sp.wait_ge(k_proj.bank_ready, 8)
            q_proj.sp(sp)
            k_proj.done(sp)
            sp.dma_start(dram["o_mk"], mkT[:, 0]).then_inc(stored, 16)
            sp.wait_ge(v_copied, 4)
            sp.dma_start(dram["o_mv"], mv[:, 0]).then_inc(stored, 16)
            sp.wait_ge(q_proj.bank_ready, 8 * NG)
            o_proj.sp(sp)
            sp.wait_ge(o_proj.bank_ready, 8 * NG)
            f_proj.sp(sp)
            o_proj.done(sp)
            sp.dma_start(dram["s_h"], h[:, :, :]).then_inc(stored, 16)
            sp.wait_ge(norm_f.normed, NORMED)
            sp.dma_start(dram["s_xn"], oT[:, :, :]).then_inc(stored, 16)
            sp.wait_ge(stored, 64)

        @block.tensor
        def _(pe):
            pe.wait_ge(loaded, 32)
            pe.wait_ge(set_, 1)
            out_proj.pe(pe)
            pe.wait_ge(mem_loaded, 64)
            norm_m.pe(pe)
            pe.wait_ge(norm_m.normed, NORMED)
            out_proj.done(pe)
            k_proj.pe(pe)
            k_proj.done(pe)
            for i in range(4):
                for k in range(KD):
                    mm = pe.matmul(ps[:, i, :], memT[:, k, (i // 2) * P:(i // 2 + 1) * P],
                                   wmv[:, k, (i % 2) * 512:(i % 2 + 1) * 512],
                                   start=(k == 0), stop=(k == KD - 1))
                mm.then_inc(v_ready, 1)
            pe.wait_ge(v_copied, 4)
            norm_q.pe(pe)
            pe.wait_ge(norm_q.normed, NORMED)
            q_proj.pe(pe)
            q_proj.done(pe)

            def scores(u):
                t, m = units[u]
                M, side = rows_of(t), t // 8
                if u >= 2:
                    pe.wait_ge(s_exp, u - 1)
                for i in range(2):
                    mm = pe.matmul(ps[0:M, u % 2, 0:N_MEM], pq[:, 2 * m + i, q_cols(t)],
                                   mkT[:, side, 2 * m + i, :], start=(i == 0), stop=(i == 1))
                mm.then_inc(s_ready, 1)

            scores(0)
            for u, (t, m) in enumerate(units):
                M, side = rows_of(t), t // 8
                if u + 1 < len(units):
                    scores(u + 1)
                pe.wait_ge(s_norm, u + 1)
                if u >= 2:
                    pe.wait_ge(t_copied, u - 1)
                for i in range(2):
                    mm = pe.transpose(ps[:, 2 + u % 2, i * P:i * P + M], prn[0:M, u % 2, i * P:(i + 1) * P],
                                      ident[0:M, 0:M])
                mm.then_inc(t_ready, 1)
                pe.wait_ge(t_copied, u + 1)
                if u >= 2:
                    pe.wait_ge(a_copied, u - 1)
                for c in range(2):
                    for i in range(2):
                        mm = pe.matmul(ps[:, 4 + u % 2, c * P:c * P + M],
                                       mv[:, side, i, m * MHD + c * P:m * MHD + (c + 1) * P],
                                       pt[:, u % 2, i, 0:M], start=(i == 0), stop=(i == 1))
                mm.then_inc(a_ready, 1)
            pe.wait_ge(a_copied, len(units))
            o_proj.pe(pe)
            o_proj.done(pe)
            norm_f.pe(pe)
            pe.wait_ge(norm_f.normed, NORMED)
            f_proj.pe(pe)

        @block.scalar
        def _(act):
            act.wait_ge(mem_loaded, 64)
            act.wait_ge(set_, 1)
            norm_m.act(act, eps)
            for i in range(4):
                act.wait_ge(v_ready, i + 1)
                act.activation(mv[:, 0, i // 2, (i % 2) * 512:(i % 2 + 1) * 512], ps[:, i, :],
                               ACT.Copy).then_inc(v_copied, 1)
            out_proj.done(act)
            norm_q.act(act, eps)
            q_proj.out(act, lambda m, bank, a, n: act.activation(pq[:, m, a:a + n], bank, ACT.Copy,
                                                                 scale=MHD ** -0.5))
            for u, (t, m) in enumerate(units):
                M = rows_of(t)
                act.wait_ge(s_max, u + 1)
                if u >= 2:
                    act.wait_ge(s_norm, u - 1)
                act.activation(pr[0:M, u % 2, :], ps[0:M, u % 2, 0:N_MEM], ACT.Exp,
                               bias=nmax[0:M, u % 2:u % 2 + 1],
                               accum_out=rsum[0:M, u % 2:u % 2 + 1]).then_inc(s_exp, 1)
                act.wait_ge(t_ready, u + 1)
                if u >= 2:
                    act.wait_ge(a_ready, u - 1)
                act.activation(pt[:, u % 2, :, 0:M],
                               ps[:, 2 + u % 2, 0:N_MEM].rearrange("p (i m) -> p i m", i=2)[:, :, 0:M],
                               ACT.Copy).then_inc(t_copied, 1)
            o_proj.done(act)
            norm_f.act(act, eps)
            f_proj.out(act, lambda m, bank, a, n: act.activation(pq[:, m, a:a + n], bank, ACT.Copy))

        @block.vector
        def _(dve):
            dve.memset(ones[:, :], 1.0).then_inc(set_, 1)
            dve.wait_ge(loaded, 32)

            def add_h(m, bank, a, n):
                return dve.tensor_tensor(h[:, m, a:a + n], bank, h[:, m, a:a + n], ALU.add)

            out_proj.out(dve, add_h)
            norm_m.dve(dve)
            k_proj.out(dve, lambda m, bank, a, n: dve.tensor_copy(mkT[:, 0, m, :], bank))
            norm_q.dve(dve)

            def row_max(u):
                M = rows_of(units[u][0])
                dve.wait_ge(s_ready, u + 1)
                if u >= 2:
                    dve.wait_ge(s_exp, u - 1)
                dve.tensor_reduce(nmax[0:M, u % 2:u % 2 + 1], ps[0:M, u % 2, 0:N_MEM], AX.X, ALU.max,
                                  negate=True).then_inc(s_max, 1)

            row_max(0)
            for u, (t, m) in enumerate(units):
                M = rows_of(t)
                if u + 1 < len(units):
                    row_max(u + 1)
                dve.wait_ge(s_exp, u + 1)
                dve.reciprocal(rinv[0:M, u % 2:u % 2 + 1], rsum[0:M, u % 2:u % 2 + 1]).then_inc(s_inv, 1)
                dve.wait_ge(s_inv, u + 1)
                if u >= 2:
                    dve.wait_ge(t_ready, u - 1)
                dve.tensor_scalar(prn[0:M, u % 2, :], pr[0:M, u % 2, :], rinv[0:M, u % 2:u % 2 + 1], None,
                                  ALU.mult).then_inc(s_norm, 1)
                dve.wait_ge(a_ready, u + 1)
                dve.tensor_copy(oT[:, 2 * m:2 * m + 2, q_cols(t)],
                                ps[:, 4 + u % 2, 0:2 * P].rearrange("p (c m) -> p c m", c=2)[:, :, 0:M]
                                ).then_inc(a_copied, 1)
            o_proj.out(dve, add_h)
            norm_f.dve(dve)


def route(nc, sem, dram, keep):
    with ExitStack() as ctx:
        def sb(name, shape, dt=F32):
            return ctx.enter_context(nc.sbuf_tensor(f"r_{name}", shape, dt))

        con, ident, pq = keep["con"], keep["ident"], keep["pq"]
        routes = keep["routes"]
        keys = sb("keys", [P, 16, NKEY])
        s = sb("s", [P, 2, 16, NKEY])
        rep = sb("rep", [P, 16, NKEY])
        v = sb("v", [P, PH, 2, PK])
        iu = sb("iu", [P, PH, 2, PK], U32)
        fi = sb("fi", [P, PH, 2, PK])
        cand = sb("cand", [P, PH, PK, PK])
        crep = sb("crep", [P, PH, PK, PK])
        sv = sb("sv", [P, PH, PK])
        si = sb("si", [P, PH, PK], U32)
        sab = sb("sab", [P, 2, PH, PK], U32)
        sabf = sb("sabf", [P, 2, PH, PK])
        num = sb("num", [P, 3, PH, PK])
        dd = sb("dd", [P, PH, PK])
        eg = sb("eg", [P, PH, PK])
        gs = sb("gs", [P, PH])
        gi = sb("gi", [P, PH])
        ps = ctx.enter_context(nc.psum_tensor("r_ps", [P, 4, 512], F32))
        x_ps = ctx.enter_context(nc.psum_tensor("r_x_ps", [P, 3, P], F32))
        loaded, s_ready, s_copied = sem("r_loaded"), sem("r_s_ready"), sem("r_s_copied")
        step = sem("r_step")
        num_ready = sem("r_num_ready")
        expd = sem("r_expd")
        turned, kept = sem("r_turned"), sem("r_kept")
        STEPS = 14
        block = ctx.enter_context(nc.Block())

        @block.sync
        def _(sp):
            sp.dma_start(keys[:, :, :], dram["keys"]).then_inc(loaded, 16)

        @block.tensor
        def _(pe):
            pe.wait_ge(loaded, 16)

            def turn(t):
                M = rows_of(t)
                pe.wait_ge(num_ready, t + 1)
                if t >= 1:
                    pe.wait_ge(kept, t)
                for i in range(3):
                    mm = pe.transpose(x_ps[:, i, 0:M], num[0:M, i].rearrange("p h k -> p (h k)"),
                                      ident[0:M, 0:M])
                mm.then_inc(turned, 1)

            for t in range(QT):
                M = rows_of(t)
                if t >= 1:
                    pe.wait_ge(s_copied, t)
                for c in range(16):
                    mm = pe.matmul(ps[0:M, c // 4, (c % 4) * P:(c % 4 + 1) * P], pq[:, c, q_cols(t)],
                                   keys[:, c, :], start=True, stop=True)
                mm.then_inc(s_ready, 1)
                if t >= 1:
                    turn(t - 1)
            turn(QT - 1)

        def keep_routes(act, t):
            M = rows_of(t)
            act.wait_ge(turned, t + 1)
            act.activation(routes[:, :, q_cols(t)], x_ps[:, :, 0:M], ACT.Copy).then_inc(kept, 1)

        @block.scalar
        def _(act):
            for t in range(QT):
                M = rows_of(t)
                act.wait_ge(s_ready, t + 1)
                if t >= 2:
                    act.wait_ge(step, STEPS * (t - 1))
                for b in range(4):
                    op = act.activation(s[0:M, t % 2, 4 * b:4 * b + 4, :].rearrange("p c n -> p (c n)"),
                                        ps[0:M, b, :], ACT.Copy)
                op.then_inc(s_copied, 1)
                if t >= 1:
                    keep_routes(act, t - 1)
                act.wait_ge(step, STEPS * t + 8)
                act.activation(eg[0:M], dd[0:M], ACT.Exp).then_inc(expd, 1)
            keep_routes(act, QT - 1)

        @block.vector
        def _(dve):
            iota16 = con[:, C_IOTA:C_IOTA + PK]

            for t in range(QT):
                M = rows_of(t)
                n_step = [STEPS * t]

                def ordered(op):
                    op.then_inc(step, 1)
                    n_step[0] += 1
                    dve.wait_ge(step, n_step[0])

                def half(x, c):
                    return x[0:M, c // 2, c % 2]

                st = s[0:M, t % 2]
                dve.wait_ge(s_copied, t + 1)
                for c in range(16):
                    op = dve.max(half(v, c)[:, 0:8], st[:, c])
                ordered(op)
                for c in range(16):
                    op = dve.match_replace(rep[0:M, c], half(v, c)[:, 0:8], st[:, c], TAKEN)
                ordered(op)
                for c in range(16):
                    dve.max(half(v, c)[:, 8:16], rep[0:M, c])
                    op = dve.max_index(half(iu, c)[:, 0:8], half(v, c)[:, 0:8], st[:, c])
                ordered(op)
                for c in range(16):
                    dve.max_index(half(iu, c)[:, 8:16], half(v, c)[:, 8:16], rep[0:M, c])
                op = dve.tensor_tensor(cand[0:M],
                                       v[0:M, :, 0, :].unsqueeze(3).broadcast_to([M, PH, PK, PK]),
                                       v[0:M, :, 1, :].unsqueeze(2).broadcast_to([M, PH, PK, PK]), ALU.add)
                ordered(op)
                def flat(x, h):
                    return x[0:M, h].rearrange("p a b -> p (a b)")

                dve.tensor_copy(fi[0:M], iu[0:M])
                for h in range(PH):
                    op = dve.max(sv[0:M, h, 0:8], flat(cand, h))
                ordered(op)
                for h in range(PH):
                    op = dve.match_replace(flat(crep, h), sv[0:M, h, 0:8], flat(cand, h), TAKEN)
                ordered(op)
                for h in range(PH):
                    dve.max(sv[0:M, h, 8:16], flat(crep, h))
                    op = dve.max_index(si[0:M, h, 0:8], sv[0:M, h, 0:8], flat(cand, h))
                ordered(op)
                for h in range(PH):
                    dve.max_index(si[0:M, h, 8:16], sv[0:M, h, 8:16], flat(crep, h))
                if t >= 1:
                    dve.wait_ge(expd, t)
                op = dve.tensor_tensor(dd[0:M], sv[0:M], sv[0:M, :, 0:1].broadcast_to([M, PH, PK]), ALU.subtract)
                ordered(op)
                dve.tensor_scalar(sab[0:M, 0], si[0:M], 4, None, ALU.logical_shift_right)
                ordered(dve.tensor_scalar(sab[0:M, 1], si[0:M], 15, None, ALU.bitwise_and))
                ordered(dve.tensor_copy(sabf[0:M], sab[0:M]))
                pick = (cand, crep)
                for i in range(2):
                    op = dve.tensor_tensor(pick[i][0:M],
                                           iota16[0:M].unsqueeze(1).unsqueeze(1).broadcast_to([M, PH, PK, PK]),
                                           sabf[0:M, i].unsqueeze(3).broadcast_to([M, PH, PK, PK]), ALU.is_equal)
                ordered(op)
                for i in range(2):
                    op = dve.tensor_tensor(pick[i][0:M], pick[i][0:M],
                                           fi[0:M, :, i, :].unsqueeze(2).broadcast_to([M, PH, PK, PK]), ALU.mult)
                ordered(op)
                if t >= 1:
                    dve.wait_ge(turned, t)
                for i in range(2):
                    dve.tensor_reduce(num[0:M, i], pick[i][0:M], AX.X, ALU.add)
                dve.wait_ge(expd, t + 1)
                ordered(dve.tensor_reduce(gs[0:M], eg[0:M], AX.X, ALU.add))
                ordered(dve.reciprocal(gi[0:M], gs[0:M]))
                dve.tensor_tensor(num[0:M, 2], eg[0:M], gi[0:M].unsqueeze(2).broadcast_to([M, PH, PK]),
                                  ALU.mult).then_inc(num_ready, 1)


TB = 132
TI = 12


def spread_gates(nc, sem, dram, keep):
    with ExitStack() as ctx:
        con, routes = keep["con"], keep["routes"]
        iota = con[:, C_IOTA:C_IOTA + NKEY]
        stage = ctx.enter_context(nc.sbuf_tensor("g_stage", [P, 2, NKEY, TB], F32))
        hot1 = ctx.enter_context(nc.sbuf_tensor("g_hot1", [P, 3, 4, NKEY], F32))
        hot2 = ctx.enter_context(nc.sbuf_tensor("g_hot2", [P, 3, 4, NKEY], F32))
        ps = ctx.enter_context(nc.psum_tensor("g_ps", [P, 3, 4, NKEY], F32))
        hot_ready, summed, copied = (sem("g_" + n) for n in ("hot_ready", "summed", "copied"))
        stored = [sem(f"g_stored{b}") for b in range(2)]
        NB, NI = NT // TB, TB // TI
        block = ctx.enter_context(nc.Block())

        @block.sync
        def _(sp):
            with sp.Fori(0, NB // 2) as i:
                for b in range(2):
                    sp.wait_ge(copied, (i * 2 + b + 1) * (NI * 3) + 3)
                    sp.dma_start(dram["s_gate"][:, :, bass.ds((i * 2 + b) * TB, TB)].rearrange("a p t -> p a t"),
                                 stage[:, b]).then_inc(stored[b], 16)
            for b in range(2):
                sp.wait_ge(stored[b], 8 * NB + 16)

        @block.tensor
        def _(pe):
            pe.sem_inc(summed, 3)
            with pe.Fori(0, NT // TI) as i:
                for g in range(3):
                    pe.wait_ge(hot_ready, i * 3 + g + 1)
                    pe.wait_ge(copied, i * 3 + g + 1)
                    for x in range(4):
                        mm = pe.matmul(ps[:, g, x, :], hot2[:, g, x, :], hot1[:, g, x, :], start=True, stop=True)
                    mm.then_inc(summed, 1)

        @block.vector
        def _(dve):
            for b in range(2):
                dve.sem_inc(stored[b], 16)
            with dve.Fori(0, NT // TI) as i:
                for g in range(3):
                    dve.wait_ge(summed, i * 3 + g + 1)
                    for x in range(4):
                        tok = bass.ds(i * TI + (4 * g + x), 1)
                        dve.tensor_scalar(hot2[:, g, x, :], iota, routes[:, 1, tok], None, ALU.is_equal)
                        op = dve.tensor_scalar(hot1[:, g, x, :], iota, routes[:, 0, tok], routes[:, 2, tok],
                                               ALU.is_equal, ALU.mult)
                    op.then_inc(hot_ready, 1)

        @block.scalar
        def _(act):
            act.sem_inc(copied, 3)
            with act.Fori(0, NB // 2) as i:
                for b in range(2):
                    act.wait_ge(stored[b], (i + 1) * 16)
                    with act.Fori(0, NI) as k:
                        for g in range(3):
                            act.wait_ge(summed, ((i * 2 + b) * NI + k) * 3 + (g + 4))
                            act.activation(stage[:, b, :, bass.ds(k * TI + 4 * g, 4)],
                                           ps[:, g].rearrange("p x a -> p a x"), ACT.Copy).then_inc(copied, 1)


CG = 4


def experts(nc, sem, dram, keep):
    with ExitStack() as ctx:
        def sb(name, shape, dt=F32):
            return ctx.enter_context(nc.sbuf_tensor(f"e_{name}", shape, dt))

        eps = keep["eps"]
        xn = sb("xn", [P, KD, NT])
        y = sb("y", [P, KD, NT])
        u = sb("u", [P, CG, KD, P])
        v = sb("v", [P, CG, D])
        gate = sb("gate", [P, CG, NT])
        act_h = sb("hid", [P, 2, TG])
        wgt = sb("wgt", [P, CG, NT])
        gain = sb("gain", [P, KD])
        ones = sb("ones", [P, P])
        sq = sb("sq", [P, 2, NT])
        h_ps = ctx.enter_context(nc.psum_tensor("e_h_ps", [P, 4, 512], F32))
        y_ps = ctx.enter_context(nc.psum_tensor("e_y_ps", [P, 4, 512], F32))
        loaded, set_ = sem("e_loaded"), sem("e_set")
        u_ready, v_ready, g_ready = ([sem(f"e_{n}{c}_ready") for c in range(CG)] for n in "uvg")
        h_ready, gelued, weighed = sem("e_h_ready"), sem("e_gelued"), sem("e_weighed")
        y_ready, y_added = sem("e_y_ready"), sem("e_y_added")
        stored = sem("e_stored")
        norm = Norm(nc, sem, "e_norm", y, xn, gain, ones[:, :], sq, h_ps, sq[:, 0, :], NT)
        NGR = NKEY // CG
        NHG = CG * NG
        NY = KD * NG
        outs = [(m, g) for m in range(KD) for g in range(NG)]
        block = ctx.enter_context(nc.Block())

        @block.sync
        def _(sp):
            sp.dma_start(xn[:, :, :], dram["s_xn"]).then_inc(loaded, 16)
            sp.dma_start(y[:, :, :], dram["s_h"]).then_inc(loaded, 16)
            sp.dma_start(gain[:, :], dram["g_fin"]).then_inc(loaded, 16)
            with sp.Fori(0, NGR) as i:
                for c in range(CG):
                    sp.wait_ge(weighed, i * NHG + 2)
                    sp.dma_start(u[:, c], dram["ut"][i * CG + c]).then_inc(u_ready[c], 16)
                    sp.dma_start(gate[:, c, :], dram["s_gate"][i * CG + c]).then_inc(g_ready[c], 16)
                sp.wait_ge(y_ready, i * NY + 1)
                for c in range(CG):
                    sp.dma_start(v[:, c, :], dram["v"][i * CG + c]).then_inc(v_ready[c], 16)
            sp.wait_ge(norm.normed, NORMED)
            sp.dma_start(dram["o_y"], xn[:, :, :]).then_inc(stored, 16)
            sp.wait_ge(stored, 16)

        @block.tensor
        def _(pe):
            pe.sem_inc(h_ready, 1)
            pe.sem_inc(y_ready, 1)
            pe.wait_ge(loaded, 48)
            pe.wait_ge(set_, 1)
            with pe.Fori(0, NGR) as i:
                for c in range(CG):
                    pe.wait_ge(u_ready[c], (i + 1) * 16)
                    for g in range(NG):
                        n = NG * c + g
                        pe.wait_ge(gelued, i * NHG + n + 1)
                        for k in range(KD):
                            mm = pe.matmul(h_ps[:, n % 4, 0:TG], u[:, c, k, :], xn[:, k, g * TG:(g + 1) * TG],
                                           start=(k == 0), stop=(k == KD - 1))
                        mm.then_inc(h_ready, 1)
                for c in range(CG):
                    pe.wait_ge(v_ready[c], (i + 1) * 16)
                for b in range(0, NY, 4):
                    for c in range(CG):
                        if b == 0:
                            pe.wait_ge(weighed, i * NHG + NG * (c + 1) + 2)
                        for o in range(4):
                            m, g = outs[b + o]
                            if c == 0:
                                pe.wait_ge(y_added, i * NY + b + o + 1)
                            mm = pe.matmul(y_ps[:, o, 0:TG], v[:, c, m * P:(m + 1) * P],
                                           wgt[:, c, g * TG:(g + 1) * TG], start=(c == 0), stop=(c == CG - 1))
                            if c == CG - 1:
                                mm.then_inc(y_ready, 1)
            pe.wait_ge(y_added, NGR * NY + 4)
            norm.pe(pe)

        @block.scalar
        def _(act):
            act.sem_inc(gelued, 4)
            with act.Fori(0, NGR) as i:
                for n in range(NHG):
                    act.wait_ge(h_ready, i * NHG + n + 2)
                    act.wait_ge(weighed, i * NHG + n + 1)
                    act.activation(act_h[:, n % 2, :], h_ps[:, n % 4, 0:TG], ACT.Gelu).then_inc(gelued, 1)
            act.wait_ge(y_added, NGR * NY + 4)
            norm.act(act, eps)

        @block.vector
        def _(dve):
            dve.memset(ones[:, :], 1.0).then_inc(set_, 1)
            dve.sem_inc(weighed, 2)
            dve.sem_inc(y_added, 4)
            dve.wait_ge(loaded, 48)
            with dve.Fori(0, NGR) as i:
                for c in range(CG):
                    dve.wait_ge(g_ready[c], (i + 1) * 16)
                    for g in range(NG):
                        n = NG * c + g
                        cols = slice(g * TG, (g + 1) * TG)
                        dve.wait_ge(gelued, i * NHG + n + 5)
                        dve.wait_ge(y_ready, i * NY + 1)
                        dve.tensor_tensor(wgt[:, c, cols], act_h[:, n % 2, :], gate[:, c, cols],
                                          ALU.mult).then_inc(weighed, 1)
                for o, (m, g) in enumerate(outs):
                    cols = slice(g * TG, (g + 1) * TG)
                    dve.wait_ge(y_ready, i * NY + o + 2)
                    dve.wait_ge(y_added, i * NY + 4)
                    dve.tensor_tensor(y[:, m, cols], y_ps[:, o % 4, 0:TG], y[:, m, cols],
                                      ALU.add).then_inc(y_added, 1)
            dve.wait_ge(y_added, NGR * NY + 4)
            norm.dve(dve)


def build(nc, dram):
    with ExitStack() as ctx:
        def sem(name):
            return ctx.enter_context(nc.semaphore(name))

        keep = {"con": ctx.enter_context(nc.sbuf_tensor("con", [P, C_W], F32)),
                "eps": ctx.enter_context(nc.sbuf_tensor("eps", [P, 1], F32))}
        keep["ident"] = keep["con"][:, C_ID:C_ID + P]
        with nc.sbuf_tensor("routes", [P, 3, NT], F32) as routes:
            keep["routes"] = routes
            with nc.sbuf_tensor("oT", [P, KD, NT], F32) as oT:
                keep["oT"] = oT
                with ExitStack() as mix:
                    for name, shape, dt in (("cs", [P, 2, NT], F32), ("xn", [P, KD, NT], F32),
                                            ("vnat", [P, 10, VW], F32), ("score", [P, SC_W], F32),
                                            ("mbf", [P, MB_W // 2], F32), ("dk", [104, NK], F32),
                                            ("gb", [104, NK], F32), ("ka", [P, NK], F32),
                                            ("causal", [P, P], BF16), ("identb", [P, P], BF16)):
                        keep[name] = mix.enter_context(nc.sbuf_tensor(name, shape, dt))
                    keep["mb"] = keep["mbf"][:, :].bitcast(BF16)
                    mix_inputs(nc, sem, dram, keep)
                    attention_pairs(nc, sem, dram, keep, True)
                    attention_pairs(nc, sem, dram, keep, False)
                with nc.sbuf_tensor("pq", [P, 16, NT], F32) as pq:
                    keep["pq"] = pq
                    with nc.sbuf_tensor("h", [P, KD, NT], F32) as h:
                        keep["h"] = h
                        memory_and_mixer(nc, sem, dram, keep)
                    route(nc, sem, dram, keep)
            spread_gates(nc, sem, dram, keep)
        experts(nc, sem, dram, keep)


OUT = {"o_y": [P, KD, NT], "o_v": [NT, VW], "o_ka": [P, NK], "o_kidx": [HD, NK], "o_fk": [8, HD, NK],
       "o_logf": [8, NK], "o_mk": [P, KD, N_MEM], "o_mv": [P, 2, D]}
SCRATCH = {"s_h": [P, KD, NT], "s_xn": [P, KD, NT], "s_gate": [NKEY, P, NT]}


def constants():
    import numpy as np
    f = np.float32
    con = np.zeros((P, C_W), f)
    con[:, C_ID:C_ID + P] = np.eye(P)
    con[:, C_CAUSAL:C_CAUSAL + P] = np.where(np.arange(P)[None, :] <= np.arange(P)[:, None], 0.0, NEG)
    for m in range(P):
        d = m % HD
        if d < ROT_DIM // 2:
            con[m + ROT_DIM // 2, C_ROT + m] = -1.0
        elif d < ROT_DIM:
            con[m - ROT_DIM // 2, C_ROT + m] = 1.0
    con[:, C_IOTA:C_IOTA + NKEY] = np.arange(NKEY)[None, :]
    for h in range(8):
        con[64 + h, C_SEL + h] = con[96 + h, C_SEL + h] = 1.0
    freq = np.power(f(ROPE_THETA), -np.arange(0, ROT_DIM, 2, dtype=f) / f(ROT_DIM)).astype(f)
    pos = np.concatenate([np.arange(T_P), PAST + np.arange(T_S)]).astype(f)
    ang = (pos[:, None] * freq[None, :]).astype(f)
    cs = np.zeros((P, 2, NT), f)
    cs[:, 0] = 1.0
    for m in range(P):
        if m % HD < ROT_DIM:
            cs[m, 0] = np.cos(ang[:, (m % HD) % (ROT_DIM // 2)])
            cs[m, 1] = np.sin(ang[:, (m % HD) % (ROT_DIM // 2)])
    return con, cs


def kernel(x_prompt, x_sample, cache_dsa_k, cache_dsa_v, cache_dsa_kidx, cache_fox_k, cache_fox_v,
           cache_fox_logf, cache_mem_k, cache_mem_v, mem_prompt, norm_mix_g, w_in, b_fox_f, w_out,
           mem_norm_g, w_mem_kv, norm_mem_g, w_mem_q, w_mem_o, norm_ffn_g, peer_w_q, peer_keys1,
           peer_keys2, peer_u, peer_v, final_norm_g):
    import numpy as np
    import concourse.bacc as bacc
    from concourse.bass_utils import run_bass_kernel_spmd

    def arr(x):
        return np.asarray(x)

    def rows(w):
        return arr(w).reshape(KD, P, -1).transpose(1, 0, 2)

    def blocks(w):
        return arr(w).reshape(KD, P, -1, P).transpose(2, 1, 0, 3)

    def pairs(w):
        return w.reshape(w.shape[0], 2, 4, HD).transpose(0, 2, 1, 3).reshape(w.shape[0], 8 * HD)

    w = arr(w_in)[0]
    aq, ak, av, aqi, aki, aw, fq, fk, fv, ff = np.split(w, np.cumsum(
        [512, 128, 128, 256, 64, 4, 512, 512, 512]), axis=1)
    wo = arr(w_out)[0]
    wo = np.concatenate([pairs(wo[:512].T).T, wo[512:]], axis=0)
    con, cs = constants()
    mkv = arr(w_mem_kv)[0]
    gains = np.stack([arr(mem_norm_g)[0], arr(norm_mem_g)[0], arr(norm_ffn_g)[0]])
    data = {
        "con": con, "cs": cs,
        "xT": rows(np.concatenate([arr(x_prompt)[0], arr(x_sample)[0]]).T),
        "g_mix": arr(norm_mix_g)[0].reshape(KD, P).T, "fb": arr(b_fox_f)[0][:, None],
        "w_rope": np.stack([rows(ak), rows(aqi[:, :P]), rows(aqi[:, P:]), rows(np.concatenate([aki, aki], 1))]),
        "w_f": rows(ff), "w_v": rows(np.concatenate([fv, av, aw], 1)),
        "w_aq": blocks(pairs(aq)), "w_fq": blocks(fq), "w_fk": blocks(fk),
        "c_ka": arr(cache_dsa_k)[0, 0].reshape(PAST, P).T,
        "c_kidx": np.concatenate([arr(cache_dsa_kidx)[0, 0].T] * 2),
        "c_logf": arr(cache_fox_logf)[0, 0].T,
        "c_v": np.concatenate([arr(cache_fox_v)[0, 0].reshape(PAST, 512),
                               arr(cache_dsa_v)[0, 0].reshape(PAST, P)], 1),
        "c_fk": arr(cache_fox_k)[0, 0].reshape(PAST, 512).T.reshape(8, HD, PAST),
        "w_out": blocks(wo), "memT": rows(arr(mem_prompt)[0].T),
        "g_rest": gains.reshape(3, KD, P).transpose(2, 0, 1),
        "w_mk": blocks(mkv[:, :D]), "w_mv": rows(mkv[:, D:]),
        "w_mq": blocks(arr(w_mem_q)[0]), "w_mo": blocks(arr(w_mem_o)[0]), "w_pq": blocks(arr(peer_w_q)[0]),
        "c_mk": rows(arr(cache_mem_k)[0, 0].reshape(N_MEM, D).T),
        "c_mv": arr(cache_mem_v)[0, 0].reshape(2, P, D).transpose(1, 0, 2),
        "keys": np.stack([arr(peer_keys1)[0], arr(peer_keys2)[0]], 1).reshape(16, NKEY, P).transpose(2, 0, 1),
        "ut": arr(peer_u)[0].reshape(NKEY, P, KD, P).transpose(0, 3, 2, 1),
        "v": arr(peer_v)[0].reshape(NKEY, P, D),
        "g_fin": arr(final_norm_g).reshape(KD, P).T,
    }
    data = {k: np.ascontiguousarray(a) for k, a in data.items()}
    nc = bacc.Bacc("TRN2", target_bir_lowering=False, num_devices=1)
    dram = {k: nc.dram_tensor("in_" + k, list(a.shape), F32, kind="ExternalInput").ap() for k, a in data.items()}
    dram |= {k: nc.dram_tensor(k, s, F32, kind="ExternalOutput").ap() for k, s in OUT.items()}
    dram |= {k: nc.dram_tensor(k, s, F32, kind="Internal").ap() for k, s in SCRATCH.items()}
    build(nc, dram)
    r = run_bass_kernel_spmd(nc, [{"in_" + k: a for k, a in data.items()}], core_ids=[0]).results[0]

    y = r["o_y"].transpose(2, 1, 0).reshape(NT, D)
    v, ka, ki, lf = r["o_v"], r["o_ka"].T, r["o_kidx"].T, r["o_logf"].T
    fk = r["o_fk"].transpose(2, 0, 1).reshape(NK, 512)
    mk = r["o_mk"].transpose(2, 1, 0)
    mv = r["o_mv"].transpose(1, 0, 2)
    p, s, n = slice(0, T_P), slice(T_P + PAST, NK), slice(T_P, NT)

    def state(k, t):
        m = v[t].shape[0]
        return (ka[k].reshape(1, 1, m, 2, HD), v[t, 512:].reshape(1, 1, m, 2, HD), ki[k].reshape(1, 1, m, HD),
                fk[k].reshape(1, 1, m, 8, HD), v[t, :512].reshape(1, 1, m, 8, HD), lf[k].reshape(1, 1, m, 8))

    return (y[None, :T_P], y[None, T_P:]) + state(p, p) + (
        mk.reshape(1, 1, N_MEM, MH, MHD), mv.reshape(1, 1, N_MEM, MH, MHD)) + state(s, n)
```

```python
from contextlib import ExitStack

import concourse.bass as bass
from concourse import mybir

F32 = mybir.dt.float32
BF16 = mybir.dt.bfloat16
F32R = mybir.dt.float32r
U32 = mybir.dt.uint32
ACT = mybir.ActivationFunctionType
ALU = mybir.AluOpType
AX = mybir.AxisListType

P = 128
D = 1024
KD = D // P
T_P, T_S, PAST = 1024, 32, 128
NT = T_P + T_S
TG, NG = 352, 3
QT = 9
NK = T_P + PAST + T_S
HD = 64
VW = 640
EPS = 1e-6
NEG = -1e30
OUTSIDE = -1e38
TAKEN = -3e38
N_MEM, MH, MHD = 256, 4, 256
PH, NKEY, PK = 8, 128, 16
ROPE_THETA, ROT_DIM = 500000.0, 16

assert NT == TG * NG and NG * TG <= 1536

C_ID, C_CAUSAL, C_ROT, C_IOTA, C_SEL = 0, 128, 256, 384, 512
C_W = 520


def rows_of(t):
    return P if t < QT - 1 else T_S


def q_cols(t):
    return slice(t * P, t * P + rows_of(t))


def key_cols(t):
    return (0, P * (t + 1)) if t < QT - 1 else (T_P, PAST + T_S)


def key_blocks(t):
    return [(b, P) for b in range(t + 1)] if t < QT - 1 else [(8, P), (9, T_S)]


def groups_of(t):
    blocks = key_blocks(t)
    return [blocks[i:i + 4] for i in range(0, len(blocks), 4)]


SC_OFF = {t: sum(key_cols(s)[1] for s in range(2, t)) for t in range(2, QT)}
SC_W = sum(key_cols(s)[1] for s in range(2, QT))
MB_OFF = {t: sum(key_cols(s)[1] for s in range(t)) for t in range(QT)}
MB_W = sum(key_cols(s)[1] for s in range(QT))
UNITS = [(t, e) for t in range(QT) for e in range(2)]
NU = len(UNITS)
GROUPS_TO = [sum(len(groups_of(t)) for t, e in UNITS[:u]) for u in range(NU + 1)]
NGRP = GROUPS_TO[NU]


NORMED = KD + 5


class Norm:

    def __init__(self, nc, sem, name, src, dst, gain, ones, sq, ps, root, w):
        self.nc, self.src, self.dst, self.gain, self.ones = nc, src, dst, gain, ones
        self.sq, self.ps, self.root, self.w = sq, ps, root, w
        self.spans = [(g, g * TG, min(w - g * TG, TG)) for g in range((w + TG - 1) // TG)]
        self.squared = sem(name + "_squared")
        self.summed = sem(name + "_summed")
        self.rooted = sem(name + "_rooted")
        self.normed = sem(name + "_normed")

    def act(self, act):
        for k in range(KD):
            if k >= 2:
                act.wait_ge(self.summed, k - 1)
            act.activation(self.sq[:, k % 2, 0:self.w], self.src[:, k, 0:self.w],
                           ACT.Square).then_inc(self.squared, 1)
        act.wait_ge(self.normed, 1)
        act.activation(self.root[:, 0:self.w], self.sq[:, 1, 0:self.w], ACT.Sqrt).then_inc(self.rooted, 1)

    def pe(self, pe):
        for k in range(KD):
            pe.wait_ge(self.squared, k + 1)
            for g, a, n in self.spans:
                mm = pe.matmul(self.ps[:, g, 0:n], self.ones, self.sq[:, k % 2, a:a + n],
                               start=(k == 0), stop=(k == KD - 1))
            mm.then_inc(self.summed, 1)

    def dve(self, dve):
        root, mean = self.root[:, 0:self.w], self.sq[:, 1, 0:self.w]
        dve.wait_ge(self.summed, KD)
        for g, a, n in self.spans:
            op = dve.tensor_scalar(mean[:, a:a + n], self.ps[:, g, 0:n], 1.0 / D, EPS, ALU.mult, ALU.add)
        op.then_inc(self.normed, 1)
        dve.wait_ge(self.rooted, 1)
        dve.reciprocal(root, root).then_inc(self.normed, 1)
        dve.wait_ge(self.normed, 2)
        dve.scalar_tensor_tensor(out=mean, in0=mean, scalar=-0.5, in1=root, op0=ALU.mult,
                                 op1=ALU.mult).then_inc(self.normed, 1)
        dve.wait_ge(self.normed, 3)
        dve.tensor_tensor(mean, mean, root, ALU.mult).then_inc(self.normed, 1)
        dve.wait_ge(self.normed, 4)
        dve.scalar_tensor_tensor(out=root, in0=mean, scalar=1.5, in1=root, op0=ALU.add,
                                 op1=ALU.mult).then_inc(self.normed, 1)
        dve.wait_ge(self.normed, 5)
        for k in range(KD):
            dve.scalar_tensor_tensor(out=self.dst[:, k, 0:self.w], in0=self.src[:, k, 0:self.w],
                                     scalar=self.gain[:, k:k + 1], in1=self.root[:, 0:self.w],
                                     op0=ALU.mult, op1=ALU.mult).then_inc(self.normed, 1)


class Project:

    def __init__(self, nc, sem, name, w_dram, M, wbuf, src, ps, w):
        self.w_dram, self.M, self.wbuf, self.src, self.ps = w_dram, M, wbuf, src, ps
        self.spans = [(g, g * TG, min(w - g * TG, TG)) for g in range((w + TG - 1) // TG)]
        self.w_ready = [sem(f"{name}_w{b}_ready") for b in range(2)]
        self.bank_ready = sem(name + "_bank_ready")
        self.bank_free = sem(name + "_bank_free")

    def sp(self, sp):
        n = len(self.spans)
        for b in range(2):
            sp.dma_start(self.wbuf[:, b], self.w_dram[b]).then_inc(self.w_ready[b], 16)
        with sp.Fori(1, self.M // 2) as i:
            for b in range(2):
                sp.wait_ge(self.bank_ready, (i * 2 + b - 1) * n)
                sp.dma_start(self.wbuf[:, b], self.w_dram[i * 2 + b]).then_inc(self.w_ready[b], 16)

    def pe(self, pe):
        n = len(self.spans)
        with pe.Fori(0, self.M // 2) as i:
            for b in range(2):
                pe.wait_ge(self.w_ready[b], (i + 1) * 16)
                for g, a, c in self.spans:
                    pe.wait_ge(self.bank_free, (i * 2 + b) * n + g + 1)
                    for k in range(KD):
                        mm = pe.matmul(self.ps[:, b * n + g, 0:c], self.wbuf[:, b, k, :],
                                       self.src[:, k, a:a + c], start=(k == 0), stop=(k == KD - 1))
                    mm.then_inc(self.bank_ready, 1)

    def out(self, eng, step):
        n = len(self.spans)
        eng.sem_inc(self.bank_free, 2 * n)
        with eng.Fori(0, self.M // 2) as i:
            for b in range(2):
                for g, a, c in self.spans:
                    eng.wait_ge(self.bank_ready, (i * 2 + b) * n + g + 1)
                    step(i * 2 + b, self.ps[:, b * n + g, 0:c], a, c).then_inc(self.bank_free, 1)

    def done(self, eng):
        eng.wait_ge(self.bank_free, (self.M + 2) * len(self.spans))


def mix_inputs(nc, sem, dram, keep):
    with ExitStack() as ctx:
        def sb(name, shape, dt=F32):
            return ctx.enter_context(nc.sbuf_tensor(name, shape, dt))

        con, ident, xn = keep["con"], keep["ident"], keep["xn"]
        xT = keep["oT"]
        cos, sin = keep["cs"][:, 0, :], keep["cs"][:, 1, :]
        rot = con[:, C_ROT:C_ROT + P]
        gain = sb("a_gain", [P, KD])
        ones = sb("a_ones", [P, P])
        sq = sb("a_sq", [P, 2, NT])
        root = sq[:, 0, :]
        raw = sq
        wv = sb("a_wv", [P, KD, VW + 4])
        wrope = sb("a_wrope", [P, 2, KD, P])
        wf = sb("a_wf", [P, KD, 8])
        qi = sb("a_qi", [P, 2, NT])
        kidx = sb("a_kidx", [P, NK])
        aw = sb("a_aw", [P, QT, 4])
        relu = sq[:, 0, 0:T_P]
        spare = keep["score"]
        tmp, tmp2 = spare[:, 2 * NT:2 * NT + TG], spare[:, 2 * NT + TG:2 * NT + 2 * TG]
        zz, za = spare[64:72, 0:NT], spare[64:72, NT:2 * NT]
        fb = sb("a_fb", [72, 1])[64:72, :]
        lf = keep["mbf"][64:72, 0:NK]
        ps = ctx.enter_context(nc.psum_tensor("a_ps", [P, 8, 512], F32))

        vnat, dk, gb, ka, score = keep["vnat"], keep["dk"], keep["gb"], keep["ka"], keep["score"]

        loaded = sem("a_loaded")
        w_rope = [sem(f"a_w_rope{b}") for b in range(2)]
        ones_set = sem("a_ones_set")
        norm = Norm(nc, sem, "a_norm", xT, xn, gain, ones[:, :], sq, ps, root, NT)
        raw_ready = sem("a_raw_ready")
        raw_copied = sem("a_raw_copied")
        rot_ready = sem("a_rot_ready")
        rot_sin = sem("a_rot_sin")
        rot_cos = sem("a_rot_cos")
        roped = sem("a_roped")
        f_ready = sem("a_f_ready")
        f_step = sem("a_f_step")
        f_act = sem("a_f_act")
        v_ready = sem("a_v_ready")
        v_copied = sem("a_v_copied")
        s_ready = sem("a_s_ready")
        s_relu = sem("a_s_relu")
        s_added = sem("a_s_added")
        stored = sem("a_stored")
        scanned = sem("a_scanned")

        def rope_dst(c, g):
            a = g * TG
            if c in (1, 2):
                return [(0, TG, qi[:, c - 1, a:a + TG])]
            d = ka if c == 0 else kidx
            if g < NG - 1:
                return [(0, TG, d[:, a:a + TG])]
            m = T_P - a
            return [(0, m, d[:, a:T_P]), (m, TG - m, d[:, T_P + PAST:NK])]

        NROPE = 4
        s_units = [(t, h) for t in range(2, QT) for h in range(4)]
        block = ctx.enter_context(nc.Block())

        @block.sync
        def _(sp):
            sp.dma_start(xT[:, :, :], dram["xT"]).then_inc(loaded, 16)
            sp.dma_start(con[:, :], dram["con"]).then_inc(loaded, 16)
            sp.dma_start(keep["cs"][:, :, :], dram["cs"]).then_inc(loaded, 16)
            sp.dma_start(gain[:, :], dram["g_mix"]).then_inc(loaded, 16)
            sp.dma_start(fb, dram["fb"]).then_inc(loaded, 16)
            for b in range(2):
                sp.dma_start(wrope[:, b], dram["w_rope"][b]).then_inc(w_rope[b], 16)
            sp.dma_start(wf[:, :, :], dram["w_f"]).then_inc(loaded, 16)
            sp.dma_start(wv[:, :, :], dram["w_v"]).then_inc(loaded, 16)
            sp.dma_start(ka[:, T_P:T_P + PAST], dram["c_ka"]).then_inc(loaded, 16)
            sp.dma_start(kidx[:, T_P:T_P + PAST], dram["c_kidx"]).then_inc(loaded, 16)
            sp.dma_start(lf[:, T_P:T_P + PAST], dram["c_logf"]).then_inc(loaded, 16)
            sp.dma_start(vnat[:, 8, :], dram["c_v"]).then_inc(loaded, 16)
            for b in range(2):
                sp.wait_ge(raw_ready, NG * (b + 1))
                sp.dma_start(wrope[:, b], dram["w_rope"][2 + b]).then_inc(w_rope[b], 16)
            for t in range(QT):
                sp.wait_ge(v_copied, 3 * (t + 1))
                M = rows_of(t)
                tile = t if t < 8 else 9
                sp.dma_start(dram["o_v"][t * P:t * P + M, :], vnat[0:M, tile, :]).then_inc(stored, 16)
            sp.wait_ge(roped, NG * NROPE)
            sp.dma_start(dram["o_ka"], ka[:, :]).then_inc(stored, 16)
            sp.dma_start(dram["o_kidx"], kidx[0:HD, :]).then_inc(stored, 16)
            sp.wait_ge(f_step, 5)
            sp.dma_start(dram["o_logf"], lf[:, :]).then_inc(stored, 16)
            sp.wait_ge(stored, 16 * (QT + 3))

        @block.tensor
        def _(pe):
            pe.wait_ge(loaded, 176)
            pe.wait_ge(ones_set, 1)
            norm.pe(pe)
            pe.wait_ge(norm.normed, NORMED)
            pe.wait_ge(norm.rooted, 1)

            def project(c):
                pe.wait_ge(w_rope[c % 2], 16 * (c // 2 + 1))
                if c >= 2:
                    pe.wait_ge(raw_copied, NG * (c - 1))
                for g in range(NG):
                    for k in range(KD):
                        mm = pe.matmul(ps[:, 3 * (c % 2) + g, 0:TG], wrope[:, c % 2, k, :],
                                       xn[:, k, g * TG:(g + 1) * TG], start=(k == 0), stop=(k == KD - 1))
                    mm.then_inc(raw_ready, 1)

            def rotate(c):
                for g in range(NG):
                    n = NG * c + g
                    pe.wait_ge(raw_copied, n + 1)
                    if n >= 2:
                        pe.wait_ge(rot_sin, n - 1)
                    pe.matmul(ps[:, 6 + n % 2, 0:TG], rot, raw[:, c % 2, g * TG:(g + 1) * TG],
                              start=True, stop=True).then_inc(rot_ready, 1)

            project(0)
            for c in range(1, NROPE):
                project(c)
                rotate(c - 1)
            pe.wait_ge(raw_copied, NG * 3)
            for g in range(NG):
                for k in range(KD):
                    mm = pe.matmul(ps[0:8, g, 0:TG], wf[:, k, :], xn[:, k, g * TG:(g + 1) * TG],
                                   start=(k == 0), stop=(k == KD - 1))
                mm.then_inc(f_ready, 1)
            rotate(NROPE - 1)
            for t in range(QT):
                M, b = rows_of(t), 2 * (t % 2)
                if t < 2:
                    pe.wait_ge(f_step, 1)
                    pe.wait_ge(raw_copied, NG * NROPE)
                else:
                    pe.wait_ge(v_copied, 3 * (t - 1))
                for a, n, bank in ((0, 512, b), (512, VW + 4 - 512, b + 1)):
                    for k in range(KD):
                        mm = pe.matmul(ps[0:M, bank, 0:n], xn[:, k, q_cols(t)], wv[:, k, a:a + n],
                                       start=(k == 0), stop=(k == KD - 1))
                mm.then_inc(v_ready, 1)
            pe.wait_ge(roped, NG * NROPE)
            for u, (t, h) in enumerate(s_units):
                M, b, r = rows_of(t), 4 + 2 * (u % 2), HD * (h % 2)
                if u < 2:
                    pe.wait_ge(rot_sin, NG * NROPE)
                else:
                    pe.wait_ge(s_relu, u - 1)
                first, count = key_cols(t)
                for a in range(0, count, 512):
                    n = min(512, count - a)
                    mm = pe.matmul(ps[0:M, b + a // 512, 0:n], qi[r:r + HD, h // 2, q_cols(t)],
                                   kidx[r:r + HD, first + a:first + a + n], start=True, stop=True)
                mm.then_inc(s_ready, 1)

        @block.scalar
        def _(act):
            act.wait_ge(loaded, 176)
            act.wait_ge(ones_set, 1)
            norm.act(act)
            for c in range(NROPE):
                for g in range(NG):
                    act.wait_ge(raw_ready, NG * c + g + 1)
                    if c < 2:
                        act.wait_ge(norm.normed, NORMED)
                    if c >= 2:
                        act.wait_ge(roped, NG * (c - 2) + g + 1)
                    act.activation(raw[:, c % 2, g * TG:(g + 1) * TG], ps[:, 3 * (c % 2) + g, 0:TG],
                                   ACT.Copy).then_inc(raw_copied, 1)
            act.wait_ge(f_step, 3)
            act.activation(zz[:, :], zz[:, :], ACT.Exp, scale=-1.0).then_inc(f_act, 1)
            act.wait_ge(f_act, 1)
            act.activation(zz[:, :], zz[:, :], ACT.Ln, bias=1.0).then_inc(f_act, 1)
            act.wait_ge(ones_set, 8)
            for t in range(QT):
                act.wait_ge(v_ready, t + 1)
                M, b, tile = rows_of(t), 2 * (t % 2), t if t < 8 else 9
                act.activation(vnat[0:M, tile, 0:512], ps[0:M, b, 0:512], ACT.Copy).then_inc(v_copied, 1)
                act.activation(vnat[0:M, tile, 512:VW], ps[0:M, b + 1, 0:VW - 512],
                               ACT.Copy).then_inc(v_copied, 1)
                act.activation(aw[0:M, t, :], ps[0:M, b + 1, VW - 512:VW - 508], ACT.Copy).then_inc(v_copied, 1)
            for u, (t, h) in enumerate(s_units):
                M, b = rows_of(t), 4 + 2 * (u % 2)
                count = key_cols(t)[1]
                act.wait_ge(s_ready, u + 1)
                if u >= 1:
                    act.wait_ge(s_added, u)
                src = ps[0:M, b:b + 2, :].rearrange("p a b -> p (a b)")[:, 0:count]
                act.activation(relu[0:M, 0:count], src, ACT.Relu).then_inc(s_relu, 1)

        @block.vector
        def _(dve):
            dve.memset(ones[:, :], 1.0).then_inc(ones_set, 1)
            dve.memset(dk[64:104, :], 0.0).then_inc(ones_set, 1)
            dve.memset(gb[64:104, :], 0.0).then_inc(ones_set, 1)
            dve.wait_ge(ones_set, 3)
            dve.memset(dk[96:104, :], 1.0).then_inc(ones_set, 1)
            dve.memset(gb[64:72, :], 1.0).then_inc(ones_set, 1)
            dve.memset(vnat[:, 9, :], 0.0).then_inc(ones_set, 1)
            dve.wait_ge(loaded, 176)
            dve.tensor_copy(keep["causal"][:, :], con[:, C_CAUSAL:C_CAUSAL + P]).then_inc(ones_set, 1)
            dve.tensor_copy(keep["identb"][:, :], ident).then_inc(ones_set, 1)
            norm.dve(dve)

            def combine(c):
                for g in range(NG):
                    n = NG * c + g
                    cols = slice(g * TG, (g + 1) * TG)
                    dve.wait_ge(rot_ready, n + 1)
                    if n >= 1:
                        dve.wait_ge(roped, n)
                    dve.tensor_tensor(tmp[:, :], ps[:, 6 + n % 2, 0:TG], sin[:, cols],
                                      ALU.mult).then_inc(rot_sin, 1)
                    dve.tensor_tensor(tmp2[:, :], raw[:, c % 2, cols], cos[:, cols],
                                      ALU.mult).then_inc(rot_cos, 1)
                    dve.wait_ge(rot_sin, n + 1)
                    dve.wait_ge(rot_cos, n + 1)
                    for a, m, d in rope_dst(c, g):
                        op = dve.tensor_tensor(d, tmp[:, a:a + m], tmp2[:, a:a + m], ALU.add)
                    op.then_inc(roped, 1)

            for c in range(NROPE - 1):
                combine(c)
            dve.wait_ge(f_ready, NG)
            for g in range(NG):
                op = dve.tensor_scalar(za[:, g * TG:(g + 1) * TG], ps[0:8, g, 0:TG], fb[:, 0:1], None, ALU.add)
            op.then_inc(f_step, 1)
            dve.wait_ge(f_step, 1)
            dve.tensor_scalar(zz[:, :], za[:, :], -1.0, None, ALU.mult).then_inc(f_step, 1)
            dve.wait_ge(f_step, 2)
            dve.tensor_tensor(zz[:, :], zz[:, :], za[:, :], ALU.max).then_inc(f_step, 1)
            combine(NROPE - 1)
            dve.wait_ge(f_act, 2)
            dve.scalar_tensor_tensor(out=lf[:, 0:T_P], in0=za[:, 0:T_P], scalar=0.0, in1=zz[:, 0:T_P],
                                     op0=ALU.min, op1=ALU.subtract).then_inc(f_step, 1)
            dve.scalar_tensor_tensor(out=lf[:, T_P + PAST:NK], in0=za[:, T_P:NT], scalar=0.0,
                                     in1=zz[:, T_P:NT], op0=ALU.min, op1=ALU.subtract).then_inc(f_step, 1)
            dve.wait_ge(f_step, 5)
            dve.wait_ge(ones_set, 8)
            for a, b in ((0, T_P), (T_P, NK)):
                dve.tensor_tensor_scan(dk[64:72, a:b], gb[64:72, a:b], lf[:, a:b], 0.0,
                                       ALU.mult, ALU.add).then_inc(scanned, 1)
            dve.wait_ge(scanned, 2)
            dve.tensor_scalar(gb[96:104, :], dk[64:72, :], -1.0, None, ALU.mult).then_inc(scanned, 1)
            dve.wait_ge(v_copied, 3 * QT)
            for u, (t, h) in enumerate(s_units):
                M, count = rows_of(t), key_cols(t)[1]
                dve.wait_ge(s_relu, u + 1)
                dst = score[0:M, SC_OFF[t]:SC_OFF[t] + count]
                if h == 0:
                    op = dve.tensor_scalar(dst, relu[0:M, 0:count], aw[0:M, t, 0:1], None, ALU.mult)
                else:
                    dve.wait_ge(s_added, u)
                    op = dve.scalar_tensor_tensor(out=dst, in0=relu[0:M, 0:count], scalar=aw[0:M, t, h:h + 1],
                                                  in1=dst, op0=ALU.mult, op1=ALU.add)
                op.then_inc(s_added, 1)
            dve.wait_ge(s_added, len(s_units))
            for t in range(2, QT - 1):
                dve.memset(score[0:HD, SC_OFF[t] + P * t + HD:SC_OFF[t] + P * (t + 1)], OUTSIDE)


def attention_pairs(nc, sem, dram, keep, fox):
    tag = "f" if fox else "d"
    with ExitStack() as ctx:
        def sb(name, shape, dt=F32):
            return ctx.enter_context(nc.sbuf_tensor(f"{tag}_{name}", shape, dt))

        def S(name):
            return sem(f"{tag}_{name}")

        con, ident, xn, oT = keep["con"], keep["ident"], keep["xn"], keep["oT"]
        vnat, dk, gb, score, mb = keep["vnat"], keep["dk"], keep["gb"], keep["score"], keep["mb"]
        cos, sin = keep["cs"][:, 0, :], keep["cs"][:, 1, :]
        w = sb("w", [P, 2 if fox else 1, KD, P])
        q = sb("q", [P, 2, NT]) if fox else sb("q", [P, NT])
        k = sb("k", [P, 2, NK]) if fox else keep["ka"]
        raw = None if fox else sb("raw", [P, NT])
        tmp = None if fox else sb("tmp", [P, TG])
        tmp2 = None if fox else sb("tmp2", [P, TG])
        pr = sb("p", [P, 2, T_P])
        pt = sb("pt", [P, 2, 8, P])
        opair = sb("opair", [P, 2, P])
        nmax = sb("nmax", [P, 2])
        rsum = sb("rsum", [P, 2])
        rinv = sb("rinv", [P, 2])
        best = sb("best", [P, QT, 8]) if fox else None
        s_ps = ctx.enter_context(nc.psum_tensor(f"{tag}_s_ps", [P, 4, 512], F32))
        t_ps = ctx.enter_context(nc.psum_tensor(f"{tag}_t_ps", [P, 2, 4, P], F32))
        o_ps = ctx.enter_context(nc.psum_tensor(f"{tag}_o_ps", [P, 2, 512], F32))
        x_ps = o_ps[:, 1, P:2 * P]

        NP_ = 6
        w_ready = S("w_ready")
        p_ready, p_copied = S("proj_ready"), S("proj_copied")
        if fox:
            bh_ready, store = S("bias_rows_ready"), S("k_stored")
            picked, dropped, masked = S("picked"), S("dropped"), S("masked")
        else:
            roped, rsin, rcos = S("roped"), S("rot_sin"), S("rot_cos")
        qk_ready, max_ready, p_exp = S("qk_ready"), S("max_ready"), S("exp_done")
        pt_ready, pt_copied = S("pt_ready"), S("pt_copied")
        pv_ready, o_inv, o_normed = S("pv_ready"), S("o_inv"), S("o_normed")
        x_ready, x_copied = S("x_ready"), S("x_copied")
        passed = S("passed")
        n_w = 4 if fox else 1
        copies = 6 if fox else 3

        block = ctx.enter_context(nc.Block())

        @block.sync
        def _(sp):
            with sp.Fori(0, 4) as j:
                sp.wait_ge(p_ready, j * NP_ + 1)
                if fox:
                    sp.wait_ge(qk_ready, j * NU + 1)
                    sp.dma_start(w[:, 0], dram["w_fq"][j]).then_inc(w_ready, 16)
                    sp.dma_start(w[:, 1], dram["w_fk"][j]).then_inc(w_ready, 16)
                    for e in range(2):
                        sp.dma_start(k[0:HD, e, T_P:T_P + PAST], dram["c_fk"][j * 2 + e]).then_inc(w_ready, 16)
                    sp.wait_ge(p_copied, j * copies + copies)
                    for e in range(2):
                        sp.dma_start(dram["o_fk"][j * 2 + e], k[0:HD, e, :]).then_inc(store, 16)
                else:
                    sp.dma_start(w[:, 0], dram["w_aq"][j]).then_inc(w_ready, 16)
            if fox:
                sp.wait_ge(store, 32 * 4 + 16)

        @block.tensor
        def _(pe):
            pe.sem_inc(p_ready, 1)
            pe.sem_inc(qk_ready, 1)
            pe.sem_inc(x_ready, 2)
            pe.sem_inc(pt_ready, 1)

            def project(j, r, wi, g):
                for kk in range(KD):
                    mm = pe.matmul(s_ps[:, r % 4, 0:TG], w[:, wi, kk, :], xn[:, kk, g * TG:(g + 1) * TG],
                                   start=(kk == 0), stop=(kk == KD - 1))
                mm.then_inc(p_ready, 1)

            def scores(j, u):
                t, e = UNITS[u]
                M, r = rows_of(t), HD * e
                first, count = key_cols(t)
                pe.wait_ge(p_exp, j * NU + u + 1)
                settled(t)
                for a in range(0, count, 512):
                    n = min(512, count - a)
                    dst = s_ps[0:M, 2 * (u % 2) + a // 512, 0:n]
                    last = a + n == count
                    if fox:
                        mm = pe.matmul(dst, q[0:104, e, q_cols(t)], k[0:104, e, first + a:first + a + n],
                                       start=True, stop=not last)
                        if last:
                            m = min(P, M)
                            mm = pe.matmul(dst[:, n - m:n], keep["identb"][0:M, 0:M], keep["causal"][0:M, 0:m],
                                           start=False, stop=True)
                    else:
                        pe.matmul(dst, q[r:r + HD, q_cols(t)], k[r:r + HD, first + a:first + a + n],
                                  start=True, stop=False)
                        mm = pe.matmul(dst, keep["identb"][0:M, 0:M],
                                       mb[0:M, MB_OFF[t] + a:MB_OFF[t] + a + n], start=False, stop=True)
                mm.then_inc(qk_ready, 1)

            def settled(t):
                if t == QT - 1:
                    pe.sem_inc(passed, 1)

            def head_out(j, t):
                M = rows_of(t)
                pe.wait_ge(o_normed, j * NU + 2 * t + 4)
                pe.wait_ge(x_copied, j * QT + t + 1)
                settled(t)
                pe.transpose(x_ps[:, 0:M], opair[0:M, t % 2, :], ident[0:M, 0:M]).then_inc(x_ready, 1)

            with pe.Fori(0, 4) as j:
                pe.wait_ge(w_ready, (j + 1) * (16 * n_w))
                pe.wait_ge(p_exp, j * NU + 2)
                if fox:
                    for r in range(6):
                        if r >= 4:
                            pe.wait_ge(p_copied, j * copies + r - 3)
                        project(j, r, r // 3, r % 3)
                    pe.wait_ge(p_copied, (j + 1) * copies)
                    pe.wait_ge(bh_ready, j * 2 + 4)
                else:
                    for g in range(NG):
                        project(j, g, 0, g)
                    for g in range(NG):
                        pe.wait_ge(p_copied, j * copies + g + 1)
                        if g == 2:
                            pe.wait_ge(p_copied, j * copies + 2)
                        bank = (3, 0, 1)[g]
                        pe.matmul(s_ps[:, bank, 0:TG], con[:, C_ROT:C_ROT + P], raw[:, g * TG:(g + 1) * TG],
                                  start=True, stop=True).then_inc(p_ready, 1)
                    pe.wait_ge(roped, (j + 1) * NG)
                def values(u):
                    t, e = UNITS[u]
                    M, nb = rows_of(t), len(key_blocks(t))
                    pe.wait_ge(o_normed, j * NU + u + 1)
                    if e == 1:
                        pe.wait_ge(x_copied, j * QT + t + 1)
                    pe.wait_ge(pt_copied, j * NGRP + GROUPS_TO[u + 1] + 2)
                    for i, (b, _) in enumerate(key_blocks(t)):
                        vc = (j * 2 + e) * HD if fox else 512 + e * HD
                        mm = pe.matmul(o_ps[0:M, u % 2, 0:HD], pt[:, u % 2, i, 0:M],
                                       vnat[:, b, bass.ds(vc, HD)], start=(i == 0), stop=(i == nb - 1))
                    mm.then_inc(pv_ready, 1)
                    if e == 0 and t >= 1:
                        head_out(j, t - 1)

                scores(j, 0)
                scores(j, 1)
                group = 0
                for u, (t, e) in enumerate(UNITS):
                    M = rows_of(t)
                    if u + 2 < NU:
                        scores(j, u + 2)
                    pe.wait_ge(p_exp, j * NU + u + 3)
                    n = 0
                    for blocks in groups_of(t):
                        pe.wait_ge(pt_copied, j * NGRP + group + 1)
                        settled(t)
                        for i, (b, kw) in enumerate(blocks):
                            mm = pe.transpose(t_ps[0:kw, group % 2, i, 0:M],
                                              pr[0:M, u % 2, P * n:P * n + kw], ident[0:M, 0:M])
                            n += 1
                        mm.then_inc(pt_ready, 1)
                        group += 1
                    if u >= 1:
                        values(u - 1)
                values(NU - 1)
                head_out(j, QT - 1)

        def tile_out(act, j, t):
            M = rows_of(t)
            act.wait_ge(x_ready, j * QT + t + 3)
            act.activation(oT[:, j + (4 if fox else 0), q_cols(t)], x_ps[:, 0:M], ACT.Copy).then_inc(x_copied, 1)

        @block.scalar
        def _(act):
            act.sem_inc(p_exp, 2)
            act.sem_inc(pt_copied, 2)
            with act.Fori(0, 4) as j:
                if fox:
                    act.wait_ge(store, j * 32 + 16)
                    for r in range(6):
                        act.wait_ge(p_ready, j * NP_ + r + 2)
                        g = r % 3
                        src = s_ps[:, r % 4, 0:TG]
                        for e in range(2):
                            half = src[e * HD:(e + 1) * HD]
                            if r < 3:
                                op = act.activation(q[0:HD, e, g * TG:(g + 1) * TG], half, ACT.Copy, scale=HD ** -0.5)
                            elif g < 2:
                                op = act.activation(k[0:HD, e, g * TG:(g + 1) * TG], half, ACT.Copy)
                            else:
                                m = T_P - g * TG
                                act.activation(k[0:HD, e, g * TG:T_P], half[:, 0:m], ACT.Copy)
                                op = act.activation(k[0:HD, e, T_P + PAST:NK], half[:, m:TG], ACT.Copy)
                        op.then_inc(p_copied, 1)
                else:
                    for g in range(NG):
                        act.wait_ge(p_ready, j * NP_ + g + 2)
                        act.activation(raw[:, g * TG:(g + 1) * TG], s_ps[:, g, 0:TG], ACT.Copy,
                                       scale=HD ** -0.5).then_inc(p_copied, 1)
                def exponentials(u):
                    t, e = UNITS[u]
                    M, count = rows_of(t), key_cols(t)[1]
                    src = s_ps[0:M, 2 * (u % 2):2 * (u % 2) + 2, :].rearrange("p a b -> p (a b)")[:, 0:count]
                    act.wait_ge(max_ready, j * NU + u + 1)
                    act.wait_ge(pt_ready, j * NGRP + GROUPS_TO[max(u - 1, 0)] + 1)
                    act.wait_ge(o_inv, j * NU + u + 1)
                    act.activation(pr[0:M, u % 2, 0:count], src, ACT.Exp, bias=nmax[0:M, u % 2:u % 2 + 1],
                                   accum_out=rsum[0:M, u % 2:u % 2 + 1]).then_inc(p_exp, 1)

                exponentials(0)
                group = 0
                for u, (t, e) in enumerate(UNITS):
                    M = rows_of(t)
                    if u + 1 < NU:
                        exponentials(u + 1)
                    act.wait_ge(pv_ready, j * NU + u + 1)
                    n = 0
                    for blocks in groups_of(t):
                        act.wait_ge(pt_ready, j * NGRP + group + 2)
                        m = len(blocks)
                        if t < QT - 1:
                            act.activation(pt[:, u % 2, n:n + m, :], t_ps[:, group % 2, 0:m, :],
                                           ACT.Copy).then_inc(pt_copied, 1)
                        else:
                            act.activation(pt[:, u % 2, 0, 0:M], t_ps[:, group % 2, 0, 0:M], ACT.Copy)
                            act.activation(pt[0:M, u % 2, 1, 0:M], t_ps[0:M, group % 2, 1, 0:M],
                                           ACT.Copy).then_inc(pt_copied, 1)
                        n += m
                        group += 1
                    if e == 1 and t >= 1:
                        tile_out(act, j, t - 1)
                tile_out(act, j, QT - 1)

        @block.vector
        def _(dve):
            dve.sem_inc(o_normed, 2)
            dve.sem_inc(x_copied, 1)
            dve.sem_inc(pv_ready, 2)
            dve.sem_inc(o_inv, 2)
            if fox:
                dve.sem_inc(store, 16)
                dve.sem_inc(dropped, 6)
                for e in range(2):
                    dve.tensor_copy(q[64:104, e, 0:T_P], dk[64:104, 0:T_P])
                    dve.tensor_copy(q[64:104, e, T_P:NT], dk[64:104, T_P + PAST:NK]).then_inc(bh_ready, 1)
                turns = [t for r in range(8) for t in range(2, QT - 1)]
                NR = len(turns)
            with dve.Fori(0, 4) as j:
                if fox:
                    for e in range(2):
                        dve.wait_ge(pv_ready, j * NU + 2)
                        dve.tensor_scalar(k[64:104, e, :], gb[64:104, :],
                                          con[64:104, bass.ds(j * 2 + (C_SEL + e), 1)],
                                          None, ALU.mult).then_inc(bh_ready, 1)
                else:
                    for g in range(NG):
                        cols = slice(g * TG, (g + 1) * TG)
                        bank = (3, 0, 1)[g]
                        dve.wait_ge(p_ready, j * NP_ + g + 5)
                        dve.tensor_tensor(tmp[:, :], s_ps[:, bank, 0:TG], sin[:, cols], ALU.mult).then_inc(rsin, 1)
                        dve.tensor_tensor(tmp2[:, :], raw[:, cols], cos[:, cols], ALU.mult).then_inc(rcos, 1)
                        dve.wait_ge(rsin, j * NG + g + 1)
                        dve.wait_ge(rcos, j * NG + g + 1)
                        dve.tensor_tensor(q[:, cols], tmp[:, :], tmp2[:, :], ALU.add).then_inc(roped, 1)
                        dve.wait_ge(roped, j * NG + g + 1)

                def row_max(u):
                    t, e = UNITS[u]
                    M, count = rows_of(t), key_cols(t)[1]
                    src = s_ps[0:M, 2 * (u % 2):2 * (u % 2) + 2, :].rearrange("p a b -> p (a b)")[:, 0:count]
                    dve.wait_ge(qk_ready, j * NU + u + 2)
                    dve.wait_ge(p_exp, j * NU + u + 1)
                    dve.tensor_reduce(nmax[0:M, u % 2:u % 2 + 1], src, AX.X, ALU.max,
                                      negate=True).then_inc(max_ready, 1)

                if fox:
                    for n_turn, tt in enumerate(turns):
                        n = key_cols(tt)[1]
                        s = score[:, SC_OFF[tt]:SC_OFF[tt] + n]
                        dve.wait_ge(dropped, j * NR + n_turn + 1)
                        dve.sem_inc(passed, 1)
                        dve.max(best[:, tt, :], s).then_inc(picked, 1)
                        dve.wait_ge(picked, j * NR + n_turn + 1)
                        dve.sem_inc(passed, 1)
                        dve.match_replace(s, best[:, tt, :], s, TAKEN).then_inc(dropped, 1)

                def normalize(u):
                    t, e = UNITS[u]
                    M = rows_of(t)
                    dve.wait_ge(pv_ready, j * NU + u + 3)
                    if e == 0:
                        dve.wait_ge(x_ready, j * QT + max(t + 1, 2))
                    dve.tensor_scalar(opair[0:M, t % 2, e * HD:(e + 1) * HD], o_ps[0:M, u % 2, 0:HD],
                                      rinv[0:M, u % 2:u % 2 + 1], None, ALU.mult).then_inc(o_normed, 1)

                row_max(0)
                row_max(1)
                for u, (t, e) in enumerate(UNITS):
                    M = rows_of(t)
                    if u + 2 < NU:
                        row_max(u + 2)
                    dve.wait_ge(p_exp, j * NU + u + 3)
                    dve.wait_ge(o_normed, j * NU + u + 1)
                    dve.reciprocal(rinv[0:M, u % 2:u % 2 + 1], rsum[0:M, u % 2:u % 2 + 1]).then_inc(o_inv, 1)
                    if u >= 1:
                        dve.wait_ge(o_inv, j * NU + u + 2)
                        normalize(u - 1)
                dve.wait_ge(o_inv, j * NU + NU + 2)
                normalize(NU - 1)

            if fox:
                dve.wait_ge(dropped, 4 * NR + 6)
                for r in range(5):
                    s = score[0:T_S, SC_OFF[8]:SC_OFF[8] + PAST + T_S]
                    dve.max(best[0:T_S, 8, :], s).then_inc(picked, 1)
                    dve.wait_ge(picked, 4 * NR + r + 1)
                    dve.match_replace(s, best[0:T_S, 8, :], s, TAKEN).then_inc(dropped, 1)
                    dve.wait_ge(dropped, 4 * NR + r + 7)
                dve.memset(mb[:, 0:MB_OFF[2]], 0.0).then_inc(masked, 1)
                dve.wait_ge(masked, 1)
                for t in range(2):
                    dve.memset(mb[0:HD, MB_OFF[t] + P * t + HD:MB_OFF[t] + P * (t + 1)], NEG)
                for t in range(2, QT):
                    M, n = rows_of(t), key_cols(t)[1]
                    dve.tensor_scalar(mb[0:M, MB_OFF[t]:MB_OFF[t] + n], score[0:M, SC_OFF[t]:SC_OFF[t] + n],
                                      -2e38, NEG, ALU.is_gt, ALU.mult)


def memory_and_mixer(nc, sem, dram, keep):
    with ExitStack() as ctx:
        def sb(name, shape, dt=F32):
            return ctx.enter_context(nc.sbuf_tensor(f"m_{name}", shape, dt))

        con, ident, oT, h, pq = (keep[n] for n in ("con", "ident", "oT", "h", "pq"))
        ones = sb("ones", [P, P])
        gains = sb("gains", [P, 3, KD])
        wbuf = sb("w", [P, 2, KD, P])
        sq = sb("sq", [P, 2, NT])
        root = sq[:, 0, :]
        mkT = sb("mkT", [P, 2, KD, N_MEM])
        mv = sb("mv", [P, 2, 2, D])
        flat = pq[:, 8:16, :].rearrange("p a b -> p (a b)")
        wmv = flat[:, 0:KD * D].rearrange("p (k n) -> p k n", k=KD)
        memT = pq[:, 0:2, :].rearrange("p a b -> p (a b)")[:, 0:KD * N_MEM].rearrange("p (k n) -> p k n", k=KD)
        pr = sb("p", [P, 2, N_MEM])
        prn = sb("pn", [P, 2, N_MEM])
        pt = sb("pt", [P, 2, 2, P])
        nmax, rsum, rinv = sb("nmax", [P, 2]), sb("rsum", [P, 2]), sb("rinv", [P, 2])
        ps = ctx.enter_context(nc.psum_tensor("m_ps", [P, 8, 512], F32))

        loaded, set_ = sem("m_loaded"), sem("m_set")
        mem_loaded = sem("m_mem_loaded")
        stored = sem("m_stored")
        v_ready, v_copied = sem("m_v_ready"), sem("m_v_copied")
        out_proj = Project(nc, sem, "m_out", dram["w_out"], 8, wbuf, oT, ps, NT)
        norm_m = Norm(nc, sem, "m_nm", memT, memT, gains[:, 0], ones[:, :], sq, ps[:, 6:8], root, N_MEM)
        k_proj = Project(nc, sem, "m_k", dram["w_mk"], 8, wbuf, memT, ps, N_MEM)
        norm_q = Norm(nc, sem, "m_nq", h, oT, gains[:, 1], ones[:, :], sq, ps, root, NT)
        q_proj = Project(nc, sem, "m_q", dram["w_mq"], 8, wbuf, oT, ps, NT)
        o_proj = Project(nc, sem, "m_o", dram["w_mo"], 8, wbuf, oT, ps, NT)
        norm_f = Norm(nc, sem, "m_nf", h, oT, gains[:, 2], ones[:, :], sq, ps, root, NT)
        f_proj = Project(nc, sem, "m_f", dram["w_pq"], 16, wbuf, oT, ps, NT)
        units = [(t, m) for t in range(QT) for m in range(MH)]
        s_ready, s_max, s_exp, s_inv, s_norm = (sem("m_" + n) for n in
                                                ("s_ready", "s_max", "s_exp", "s_inv", "s_norm"))
        t_ready, t_copied, a_ready, a_copied = (sem("m_" + n) for n in
                                                ("t_ready", "t_copied", "a_ready", "a_copied"))

        block = ctx.enter_context(nc.Block())

        @block.sync
        def _(sp):
            sp.dma_start(h[:, :, :], dram["xT"]).then_inc(loaded, 16)
            sp.dma_start(gains[:, :, :], dram["g_rest"]).then_inc(loaded, 16)
            out_proj.sp(sp)
            sp.dma_start(memT, dram["memT"]).then_inc(mem_loaded, 16)
            sp.dma_start(wmv, dram["w_mv"]).then_inc(mem_loaded, 16)
            sp.dma_start(mkT[:, 1], dram["c_mk"]).then_inc(mem_loaded, 16)
            sp.dma_start(mv[:, 1], dram["c_mv"]).then_inc(mem_loaded, 16)
            sp.wait_ge(out_proj.bank_ready, 8 * NG)
            k_proj.sp(sp)
            sp.wait_ge(k_proj.bank_ready, 8)
            q_proj.sp(sp)
            k_proj.done(sp)
            sp.dma_start(dram["o_mk"], mkT[:, 0]).then_inc(stored, 16)
            sp.wait_ge(v_copied, 4)
            sp.dma_start(dram["o_mv"], mv[:, 0]).then_inc(stored, 16)
            sp.wait_ge(q_proj.bank_ready, 8 * NG)
            o_proj.sp(sp)
            sp.wait_ge(o_proj.bank_ready, 8 * NG)
            f_proj.sp(sp)
            o_proj.done(sp)
            sp.dma_start(dram["s_h"], h[:, :, :]).then_inc(stored, 16)
            sp.wait_ge(norm_f.normed, NORMED)
            sp.dma_start(dram["s_xn"], oT[:, :, :]).then_inc(stored, 16)
            sp.wait_ge(stored, 64)

        @block.tensor
        def _(pe):
            pe.wait_ge(loaded, 32)
            pe.wait_ge(set_, 1)
            out_proj.pe(pe)
            pe.wait_ge(mem_loaded, 64)
            norm_m.pe(pe)
            pe.wait_ge(norm_m.normed, NORMED)
            out_proj.done(pe)
            k_proj.pe(pe)
            k_proj.done(pe)
            for i in range(4):
                for k in range(KD):
                    mm = pe.matmul(ps[:, i, :], memT[:, k, (i // 2) * P:(i // 2 + 1) * P],
                                   wmv[:, k, (i % 2) * 512:(i % 2 + 1) * 512],
                                   start=(k == 0), stop=(k == KD - 1))
                mm.then_inc(v_ready, 1)
            pe.wait_ge(v_copied, 4)
            norm_q.pe(pe)
            pe.wait_ge(norm_q.normed, NORMED)
            q_proj.pe(pe)
            q_proj.done(pe)

            def scores(u):
                t, m = units[u]
                M, side = rows_of(t), t // 8
                if u >= 2:
                    pe.wait_ge(s_exp, u - 1)
                for i in range(2):
                    mm = pe.matmul(ps[0:M, u % 2, 0:N_MEM], pq[:, 2 * m + i, q_cols(t)],
                                   mkT[:, side, 2 * m + i, :], start=(i == 0), stop=(i == 1))
                mm.then_inc(s_ready, 1)

            scores(0)
            for u, (t, m) in enumerate(units):
                M, side = rows_of(t), t // 8
                if u + 1 < len(units):
                    scores(u + 1)
                pe.wait_ge(s_norm, u + 1)
                if u >= 2:
                    pe.wait_ge(t_copied, u - 1)
                for i in range(2):
                    mm = pe.transpose(ps[:, 2 + u % 2, i * P:i * P + M], prn[0:M, u % 2, i * P:(i + 1) * P],
                                      ident[0:M, 0:M])
                mm.then_inc(t_ready, 1)
                pe.wait_ge(t_copied, u + 1)
                if u >= 2:
                    pe.wait_ge(a_copied, u - 1)
                for c in range(2):
                    for i in range(2):
                        mm = pe.matmul(ps[:, 4 + u % 2, c * P:c * P + M],
                                       mv[:, side, i, m * MHD + c * P:m * MHD + (c + 1) * P],
                                       pt[:, u % 2, i, 0:M], start=(i == 0), stop=(i == 1))
                mm.then_inc(a_ready, 1)
            pe.wait_ge(a_copied, len(units))
            o_proj.pe(pe)
            o_proj.done(pe)
            norm_f.pe(pe)
            pe.wait_ge(norm_f.normed, NORMED)
            f_proj.pe(pe)

        @block.scalar
        def _(act):
            act.wait_ge(mem_loaded, 64)
            act.wait_ge(set_, 1)
            norm_m.act(act)
            for i in range(4):
                act.wait_ge(v_ready, i + 1)
                act.activation(mv[:, 0, i // 2, (i % 2) * 512:(i % 2 + 1) * 512], ps[:, i, :],
                               ACT.Copy).then_inc(v_copied, 1)
            out_proj.done(act)
            norm_q.act(act)
            q_proj.out(act, lambda m, bank, a, n: act.activation(pq[:, m, a:a + n], bank, ACT.Copy,
                                                                 scale=MHD ** -0.5))
            for u, (t, m) in enumerate(units):
                M = rows_of(t)
                act.wait_ge(s_max, u + 1)
                if u >= 2:
                    act.wait_ge(s_norm, u - 1)
                act.activation(pr[0:M, u % 2, :], ps[0:M, u % 2, 0:N_MEM], ACT.Exp,
                               bias=nmax[0:M, u % 2:u % 2 + 1],
                               accum_out=rsum[0:M, u % 2:u % 2 + 1]).then_inc(s_exp, 1)
                act.wait_ge(t_ready, u + 1)
                if u >= 2:
                    act.wait_ge(a_ready, u - 1)
                act.activation(pt[:, u % 2, :, 0:M],
                               ps[:, 2 + u % 2, 0:N_MEM].rearrange("p (i m) -> p i m", i=2)[:, :, 0:M],
                               ACT.Copy).then_inc(t_copied, 1)
            o_proj.done(act)
            norm_f.act(act)
            f_proj.out(act, lambda m, bank, a, n: act.activation(pq[:, m, a:a + n], bank, ACT.Copy))

        @block.vector
        def _(dve):
            dve.memset(ones[:, :], 1.0).then_inc(set_, 1)
            dve.wait_ge(loaded, 32)

            def add_h(m, bank, a, n):
                return dve.tensor_tensor(h[:, m, a:a + n], bank, h[:, m, a:a + n], ALU.add)

            out_proj.out(dve, add_h)
            norm_m.dve(dve)
            k_proj.out(dve, lambda m, bank, a, n: dve.tensor_copy(mkT[:, 0, m, :], bank))
            norm_q.dve(dve)

            def row_max(u):
                M = rows_of(units[u][0])
                dve.wait_ge(s_ready, u + 1)
                if u >= 2:
                    dve.wait_ge(s_exp, u - 1)
                dve.tensor_reduce(nmax[0:M, u % 2:u % 2 + 1], ps[0:M, u % 2, 0:N_MEM], AX.X, ALU.max,
                                  negate=True).then_inc(s_max, 1)

            row_max(0)
            for u, (t, m) in enumerate(units):
                M = rows_of(t)
                if u + 1 < len(units):
                    row_max(u + 1)
                dve.wait_ge(s_exp, u + 1)
                dve.reciprocal(rinv[0:M, u % 2:u % 2 + 1], rsum[0:M, u % 2:u % 2 + 1]).then_inc(s_inv, 1)
                dve.wait_ge(s_inv, u + 1)
                if u >= 2:
                    dve.wait_ge(t_ready, u - 1)
                dve.tensor_scalar(prn[0:M, u % 2, :], pr[0:M, u % 2, :], rinv[0:M, u % 2:u % 2 + 1], None,
                                  ALU.mult).then_inc(s_norm, 1)
                dve.wait_ge(a_ready, u + 1)
                dve.tensor_copy(oT[:, 2 * m:2 * m + 2, q_cols(t)],
                                ps[:, 4 + u % 2, 0:2 * P].rearrange("p (c m) -> p c m", c=2)[:, :, 0:M]
                                ).then_inc(a_copied, 1)
            o_proj.out(dve, add_h)
            norm_f.dve(dve)


class EarlyHidden:

    def __init__(self, nc, sem, ctx, name, dram, xn, first, count):
        def sb(part, shape):
            return ctx.enter_context(nc.sbuf_tensor(f"{name}_{part}", shape, F32))

        self.dram, self.xn, self.first, self.count = dram, xn, first, count
        self.u, self.hid = sb("u", [P, 2, KD, P]), sb("hid", [P, 2, NT])
        self.ps = ctx.enter_context(nc.psum_tensor(name + "_ps", [P, NG, 512], F32))
        self.u_ready = [sem(f"{name}_u{b}_ready") for b in range(2)]
        self.stored = [sem(f"{name}_stored{b}") for b in range(2)]
        self.h_ready = sem(name + "_h_ready")
        self.gelued = sem(name + "_gelued")

    def load(self, sp, i, b):
        sp.wait_ge(self.h_ready, (i * 2 + b) * NG + NG)
        sp.dma_start(self.u[:, b], self.dram["ut"][i * 2 + (self.first + b)]).then_inc(self.u_ready[b], 16)

    def store(self, sp, i, b):
        sp.wait_ge(self.gelued, (i * 2 + b) * NG + 2 * NG)
        sp.dma_start(self.dram["s_hid"][i * 2 + (self.first + b)], self.hid[:, b]).then_inc(self.stored[b], 16)

    def finish(self, sp):
        for b in range(2):
            sp.wait_ge(self.stored[b], 8 * self.count + 16)

    def product(self, pe, i, b, g, k):
        if k == 0:
            if g == 0:
                pe.wait_ge(self.u_ready[b], i * 16 + 16)
            pe.wait_ge(self.gelued, (i * 2 + b) * NG + (g + 1))
        mm = pe.matmul(self.ps[:, g, 0:TG], self.u[:, b, k, :], self.xn[:, k, g * TG:(g + 1) * TG],
                       start=(k == 0), stop=(k == KD - 1))
        if k == KD - 1:
            mm.then_inc(self.h_ready, 1)

    def gelu(self, act, i, b, g):
        if g == 0:
            act.wait_ge(self.stored[b], i * 16 + 16)
        act.wait_ge(self.h_ready, (i * 2 + b) * NG + (g + 1 + 2 * NG))
        act.activation(self.hid[:, b, g * TG:(g + 1) * TG], self.ps[:, g, 0:TG],
                       ACT.Gelu).then_inc(self.gelued, 1)


def route(nc, sem, dram, keep):
    with ExitStack() as ctx:
        def sb(name, shape, dt=F32):
            return ctx.enter_context(nc.sbuf_tensor(f"r_{name}", shape, dt))

        con, ident, pq = keep["con"], keep["ident"], keep["pq"]
        routes = keep["routes"]
        keys = sb("keys", [P, 16, NKEY])
        s = sb("s", [P, 2, 16, NKEY])
        rep = sb("rep", [P, 16, NKEY])
        v = sb("v", [P, PH, 2, PK])
        iu = sb("iu", [P, PH, 2, PK], U32)
        fi = sb("fi", [P, PH, 2, PK])
        cand = sb("cand", [P, PH, PK, PK])
        crep = sb("crep", [P, PH, PK, PK])
        sv = sb("sv", [P, PH, PK])
        si = sb("si", [P, PH, PK], U32)
        sab = sb("sab", [P, 2, PH, PK], U32)
        sabf = sb("sabf", [P, 2, PH, PK])
        num = sb("num", [P, 3, PH, PK])
        dd = sb("dd", [P, PH, PK])
        eg = sb("eg", [P, PH, PK])
        gs = sb("gs", [P, PH])
        gi = sb("gi", [P, PH])
        ps = ctx.enter_context(nc.psum_tensor("r_ps", [P, 4, 512], F32))
        early = EarlyHidden(nc, sem, ctx, "r_early", dram, keep["oT"], 0, N_EARLY_R)
        tile_of = [c * QT // N_EARLY_R for c in range(N_EARLY_R)]
        halves = []
        for t in range(QT):
            cs = [c for c in range(N_EARLY_R) if tile_of[c] == t]
            halves.append((cs[:len(cs) // 2], cs[len(cs) // 2:]))
        x_ps = ctx.enter_context(nc.psum_tensor("r_x_ps", [P, 3, P], F32))
        loaded, s_ready, s_copied = sem("r_loaded"), sem("r_s_ready"), sem("r_s_copied")
        step = sem("r_step")
        num_ready = sem("r_num_ready")
        expd = sem("r_expd")
        turned, kept = sem("r_turned"), sem("r_kept")
        STEPS = 14
        block = ctx.enter_context(nc.Block())

        @block.sync
        def _(sp):
            sp.dma_start(keys[:, :, :], dram["keys"]).then_inc(loaded, 16)
            for c in range(2):
                early.load(sp, c // 2, c % 2)
            for c in range(N_EARLY_R):
                if c + 2 < N_EARLY_R:
                    early.load(sp, c // 2 + 1, c % 2)
                early.store(sp, c // 2, c % 2)
            early.finish(sp)

        @block.tensor
        def _(pe):
            pe.sem_inc(early.h_ready, 2 * NG)
            pe.wait_ge(loaded, 16)

            def turn(t):
                M = rows_of(t)
                pe.wait_ge(num_ready, t + 1)
                if t >= 1:
                    pe.wait_ge(kept, t)
                for i in range(3):
                    mm = pe.transpose(x_ps[:, i, 0:M], num[0:M, i].rearrange("p h k -> p (h k)"),
                                      ident[0:M, 0:M])
                mm.then_inc(turned, 1)

            def hidden(chunks):
                for c in chunks:
                    for g in range(NG):
                        for k in range(KD):
                            early.product(pe, c // 2, c % 2, g, k)

            for t in range(QT):
                M = rows_of(t)
                if t >= 1:
                    pe.wait_ge(s_copied, t)
                for c in range(16):
                    mm = pe.matmul(ps[0:M, c // 4, (c % 4) * P:(c % 4 + 1) * P], pq[:, c, q_cols(t)],
                                   keys[:, c, :], start=True, stop=True)
                mm.then_inc(s_ready, 1)
                hidden(halves[t][0])
                if t >= 1:
                    turn(t - 1)
                hidden(halves[t][1])
            turn(QT - 1)

        def keep_routes(act, t):
            M = rows_of(t)
            act.wait_ge(turned, t + 1)
            act.activation(routes[:, :, q_cols(t)], x_ps[:, :, 0:M], ACT.Copy).then_inc(kept, 1)

        @block.scalar
        def _(act):
            act.sem_inc(early.gelued, NG)
            for b in range(2):
                act.sem_inc(early.stored[b], 16)

            def hidden(chunks):
                for c in chunks:
                    for g in range(NG):
                        early.gelu(act, c // 2, c % 2, g)

            for t in range(QT):
                M = rows_of(t)
                act.wait_ge(s_ready, t + 1)
                if t >= 2:
                    act.wait_ge(step, STEPS * (t - 1))
                for b in range(4):
                    op = act.activation(s[0:M, t % 2, 4 * b:4 * b + 4, :].rearrange("p c n -> p (c n)"),
                                        ps[0:M, b, :], ACT.Copy)
                op.then_inc(s_copied, 1)
                hidden(halves[t][0])
                if t >= 1:
                    keep_routes(act, t - 1)
                act.wait_ge(step, STEPS * t + 8)
                act.activation(eg[0:M], dd[0:M], ACT.Exp).then_inc(expd, 1)
                hidden(halves[t][1])
            keep_routes(act, QT - 1)

        @block.vector
        def _(dve):
            iota16 = con[:, C_IOTA:C_IOTA + PK]

            for t in range(QT):
                M = rows_of(t)
                n_step = [STEPS * t]

                def ordered(op):
                    op.then_inc(step, 1)
                    n_step[0] += 1
                    dve.wait_ge(step, n_step[0])

                def half(x, c):
                    return x[0:M, c // 2, c % 2]

                st = s[0:M, t % 2]
                dve.wait_ge(s_copied, t + 1)
                for c in range(16):
                    op = dve.max(half(v, c)[:, 0:8], st[:, c])
                ordered(op)
                for c in range(16):
                    op = dve.match_replace(rep[0:M, c], half(v, c)[:, 0:8], st[:, c], TAKEN)
                ordered(op)
                for c in range(16):
                    dve.max(half(v, c)[:, 8:16], rep[0:M, c])
                    op = dve.max_index(half(iu, c)[:, 0:8], half(v, c)[:, 0:8], st[:, c])
                ordered(op)
                for c in range(16):
                    dve.max_index(half(iu, c)[:, 8:16], half(v, c)[:, 8:16], rep[0:M, c])
                op = dve.tensor_tensor(cand[0:M],
                                       v[0:M, :, 0, :].unsqueeze(3).broadcast_to([M, PH, PK, PK]),
                                       v[0:M, :, 1, :].unsqueeze(2).broadcast_to([M, PH, PK, PK]), ALU.add)
                ordered(op)
                def flat(x, h):
                    return x[0:M, h].rearrange("p a b -> p (a b)")

                dve.tensor_copy(fi[0:M], iu[0:M])
                for h in range(PH):
                    op = dve.max(sv[0:M, h, 0:8], flat(cand, h))
                ordered(op)
                for h in range(PH):
                    op = dve.match_replace(flat(crep, h), sv[0:M, h, 0:8], flat(cand, h), TAKEN)
                ordered(op)
                for h in range(PH):
                    dve.max(sv[0:M, h, 8:16], flat(crep, h))
                    op = dve.max_index(si[0:M, h, 0:8], sv[0:M, h, 0:8], flat(cand, h))
                ordered(op)
                for h in range(PH):
                    dve.max_index(si[0:M, h, 8:16], sv[0:M, h, 8:16], flat(crep, h))
                if t >= 1:
                    dve.wait_ge(expd, t)
                op = dve.tensor_tensor(dd[0:M], sv[0:M], sv[0:M, :, 0:1].broadcast_to([M, PH, PK]), ALU.subtract)
                ordered(op)
                dve.tensor_scalar(sab[0:M, 0], si[0:M], 4, None, ALU.logical_shift_right)
                ordered(dve.tensor_scalar(sab[0:M, 1], si[0:M], 15, None, ALU.bitwise_and))
                ordered(dve.tensor_copy(sabf[0:M], sab[0:M]))
                pick = (cand, crep)
                for i in range(2):
                    op = dve.tensor_tensor(pick[i][0:M],
                                           iota16[0:M].unsqueeze(1).unsqueeze(1).broadcast_to([M, PH, PK, PK]),
                                           sabf[0:M, i].unsqueeze(3).broadcast_to([M, PH, PK, PK]), ALU.is_equal)
                ordered(op)
                for i in range(2):
                    op = dve.tensor_tensor(pick[i][0:M], pick[i][0:M],
                                           fi[0:M, :, i, :].unsqueeze(2).broadcast_to([M, PH, PK, PK]), ALU.mult)
                ordered(op)
                if t >= 1:
                    dve.wait_ge(turned, t)
                for i in range(2):
                    dve.tensor_reduce(num[0:M, i], pick[i][0:M], AX.X, ALU.add)
                dve.wait_ge(expd, t + 1)
                ordered(dve.tensor_reduce(gs[0:M], eg[0:M], AX.X, ALU.add))
                ordered(dve.reciprocal(gi[0:M], gs[0:M]))
                dve.tensor_tensor(num[0:M, 2], eg[0:M], gi[0:M].unsqueeze(2).broadcast_to([M, PH, PK]),
                                  ALU.mult).then_inc(num_ready, 1)


TB = 132
TI = 12


def spread_gates(nc, sem, dram, keep):
    with ExitStack() as ctx:
        con, routes = keep["con"], keep["routes"]
        iota = con[:, C_IOTA:C_IOTA + NKEY]
        stage = ctx.enter_context(nc.sbuf_tensor("g_stage", [P, 2, NKEY, TB], F32))
        hot1 = ctx.enter_context(nc.sbuf_tensor("g_hot1", [P, 3, 4, NKEY], F32))
        hot2 = ctx.enter_context(nc.sbuf_tensor("g_hot2", [P, 3, 4, NKEY], F32))
        ps = ctx.enter_context(nc.psum_tensor("g_ps", [P, 3, 4, NKEY], F32))
        early = EarlyHidden(nc, sem, ctx, "g_early", dram, keep["oT"], N_EARLY_R, N_EARLY - N_EARLY_R)
        hot_ready, summed, copied = (sem("g_" + n) for n in ("hot_ready", "summed", "copied"))
        stored = [sem(f"g_stored{b}") for b in range(2)]
        NB, NQ = NT // TB, TB // 4
        assert N_EARLY - N_EARLY_R == 2 * NB
        products = [(b, g, k) for b in range(2) for g in range(NG) for k in range(KD)]
        after = [q * len(products) // NQ for q in range(NQ + 1)]
        block = ctx.enter_context(nc.Block())

        @block.sync
        def _(sp):
            def store_block(n, b):
                sp.wait_ge(copied, n * NQ + (NQ + 3))
                sp.dma_start(dram["s_gate"][:, :, bass.ds(n * TB, TB)].rearrange("a p t -> p a t"),
                             stage[:, b]).then_inc(stored[b], 16)

            for b in range(2):
                early.load(sp, 0, b)
            with sp.Fori(0, NB // 2 - 1) as i:
                for b in range(2):
                    for side in range(2):
                        early.load(sp, i * 2 + (b + 1), side)
                        early.store(sp, i * 2 + b, side)
                    store_block(i * 2 + b, b)
            for b in range(2):
                for side in range(2):
                    if b == 0:
                        early.load(sp, NB - 1, side)
                    early.store(sp, NB - 2 + b, side)
                store_block(NB - 2 + b, b)
            early.finish(sp)
            for b in range(2):
                sp.wait_ge(stored[b], 8 * NB + 16)

        @block.tensor
        def _(pe):
            pe.sem_inc(summed, 3)
            pe.sem_inc(early.h_ready, 2 * NG)
            with pe.Fori(0, NB) as n:
                for q in range(NQ):
                    pe.wait_ge(hot_ready, n * NQ + (q + 1))
                    pe.wait_ge(copied, n * NQ + (q + 1))
                    for x in range(4):
                        mm = pe.matmul(ps[:, q % 3, x, :], hot2[:, q % 3, x, :], hot1[:, q % 3, x, :],
                                       start=True, stop=True)
                    mm.then_inc(summed, 1)
                    for side, g, k in products[after[q]:after[q + 1]]:
                        early.product(pe, n, side, g, k)

        @block.vector
        def _(dve):
            for b in range(2):
                dve.sem_inc(stored[b], 16)
            with dve.Fori(0, NT // TI) as i:
                for g in range(3):
                    dve.wait_ge(summed, i * 3 + g + 1)
                    for x in range(4):
                        tok = bass.ds(i * TI + (4 * g + x), 1)
                        dve.tensor_scalar(hot2[:, g, x, :], iota, routes[:, 1, tok], None, ALU.is_equal)
                        op = dve.tensor_scalar(hot1[:, g, x, :], iota, routes[:, 0, tok], routes[:, 2, tok],
                                               ALU.is_equal, ALU.mult)
                    op.then_inc(hot_ready, 1)

        @block.scalar
        def _(act):
            act.sem_inc(copied, 3)
            act.sem_inc(early.gelued, NG)
            for b in range(2):
                act.sem_inc(early.stored[b], 16)
            with act.Fori(0, NB // 2) as i:
                for b in range(2):
                    act.wait_ge(stored[b], (i + 1) * 16)
                    for q in range(NQ):
                        act.wait_ge(summed, (i * 2 + b) * NQ + (q + 4))
                        act.activation(stage[:, b, :, 4 * q:4 * q + 4], ps[:, q % 3].rearrange("p x a -> p a x"),
                                       ACT.Copy).then_inc(copied, 1)
                        for side, g, k in products[after[max(q - 1, 0)]:after[q]]:
                            if k == KD - 1:
                                early.gelu(act, i * 2 + b, side, g)
                    early.gelu(act, i * 2 + b, 1, NG - 1)


N_EARLY, N_EARLY_R = 48, 32
CG = 4
HI, LO = 0, 1
PRODUCTS = ((HI, HI), (HI, LO), (LO, HI))


def experts(nc, sem, dram, keep):
    with ExitStack() as ctx:
        def sb(name, shape, dt=F32):
            return ctx.enter_context(nc.sbuf_tensor(f"e_{name}", shape, dt))

        xh = sb("xh", [P, 2, KD, NT], F32R)
        y = sb("y", [P, KD, NT])
        u = sb("u", [P, NT])
        uh = sb("uh", [P, 2, 2, KD * P], F32R)
        v = sb("v", [P, 2, D])
        vh = sb("vh", [P, CG, 2, D], F32R)
        gate = sb("gate", [P, 2, NT])
        hid = sb("hid", [P, 2, TG])
        wh = sb("wh", [P, CG, 2, NT], F32R)
        gain = sb("gain", [P, KD])
        ones = sb("ones", [P, P])
        h_ps = ctx.enter_context(nc.psum_tensor("e_h_ps", [P, NG, 512], F32))
        y_ps = ctx.enter_context(nc.psum_tensor("e_y_ps", [P, 4, 512], F32))
        loaded, set_ = sem("e_loaded"), sem("e_set")
        x_halved = sem("e_x_halved")
        passed = sem("e_passed")
        u_ready, u_rounded, u_split = sem("e_u_ready"), sem("e_u_rounded"), sem("e_u_split")
        v_ready = [sem(f"e_v{c}_ready") for c in range(2)]
        v_rounded, v_split = sem("e_v_rounded"), sem("e_v_split")
        g_ready = [sem(f"e_g{c}_ready") for c in range(2)]
        h_ready, gelued, weighed = sem("e_h_ready"), sem("e_gelued"), sem("e_weighed")
        w_rounded, w_split = sem("e_w_rounded"), sem("e_w_split")
        y_ready, y_added = sem("e_y_ready"), sem("e_y_added")
        stored = sem("e_stored")
        norm = Norm(nc, sem, "e_norm", y, y, gain, ones[:, :], gate, h_ps, gate[:, 0, :], NT)
        N_IT, NC, NL, NE = NKEY // 8, 8, 5, 3
        LIVE = {0: 0, 1: 1, 3: 2, 4: 3, 6: 4}
        EARLY = {2: 0, 5: 1, 7: 2}
        LOADS = (0, 1, 3, 2, 4, 6, 5, 7)
        SPLITS = ("u0", "u1", "v0", "v1", "u3", "v2", "v3", "u4", "u6", "v4", "v5", "v6", "v7")
        assert N_IT * NE == N_EARLY and N_IT * NL == NKEY - N_EARLY and 2 * CG == NC
        NHB = NC * NG
        NLB = NL * NG
        NY = KD * NG
        outs = [(m, g) for m in range(KD) for g in range(NG)]

        def number(i, c):
            return i * NL + (N_EARLY + LIVE[c]) if c in LIVE else i * NE + EARLY[c]

        block = ctx.enter_context(nc.Block())

        @block.sync
        def _(sp):
            sp.dma_start(y[:, :, :], dram["s_xn"]).then_inc(loaded, 16)
            sp.dma_start(gain[:, :], dram["g_fin"]).then_inc(loaded, 16)
            sp.wait_ge(x_halved, 2 * KD)
            sp.dma_start(y[:, :, :], dram["s_h"]).then_inc(loaded, 16)
            with sp.Fori(0, N_IT) as i:
                for j in range(NC):
                    sp.wait_ge(v_split, i * NC + (j + 1))
                    sp.dma_start(v[:, j % 2, :], dram["v"][number(i, j)]).then_inc(v_ready[j % 2], 16)
                    c, before = LOADS[j], LOADS[j - 1]
                    if j == 0:
                        sp.wait_ge(w_split, i * NHB + 2)
                    elif before in LIVE:
                        sp.wait_ge(u_split, i * NL + (LIVE[before] + 1))
                    else:
                        sp.wait_ge(w_split, i * NHB + ((before + 1) * NG + 2))
                    if c in LIVE:
                        sp.dma_start(u[:, 0:KD * P], dram["ut"][number(i, c)].rearrange("p k e -> p (k e)")
                                     ).then_inc(u_ready, 16)
                    else:
                        sp.dma_start(u[:, :], dram["s_hid"][number(i, c)]).then_inc(u_ready, 16)
                    sp.wait_ge(weighed, (i * NC + j) * NG + 1)
                    sp.dma_start(gate[:, j % 2, :], dram["s_gate"][number(i, j)]).then_inc(g_ready[j % 2], 16)
            sp.wait_ge(norm.normed, NORMED)
            sp.dma_start(dram["o_y"], y[:, :, :]).then_inc(stored, 16)
            sp.wait_ge(stored, 16)

        @block.tensor
        def _(pe):
            pe.sem_inc(h_ready, 1)
            pe.sem_inc(y_ready, 1)
            pe.wait_ge(x_halved, 2 * KD)
            with pe.Fori(0, N_IT) as i:
                for q in range(2):
                    for c in range(q * CG, (q + 1) * CG):
                        if c in EARLY:
                            continue
                        pe.wait_ge(u_split, i * NL + (LIVE[c] + 1))
                        for g in range(NG):
                            pe.wait_ge(gelued, i * NLB + (LIVE[c] * NG + g + 1))
                            for k in range(KD):
                                for p, (a, b) in enumerate(PRODUCTS):
                                    mm = pe.matmul(h_ps[:, g, 0:TG], uh[:, LIVE[c] % 2, a, k * P:(k + 1) * P],
                                                   xh[:, b, k, g * TG:(g + 1) * TG],
                                                   start=(k == 0 and p == 0), stop=(k == KD - 1 and p == 2))
                            mm.then_inc(h_ready, 1)
                    for b0 in range(0, NY, 4):
                        for c in range(CG):
                            if b0 == 0:
                                pe.wait_ge(v_split, i * NC + (q * CG + c + 3))
                                pe.wait_ge(w_split, i * NHB + (NG * (q * CG + c + 1) + 2))
                            for o in range(4):
                                m, g = outs[b0 + o]
                                if c == 0:
                                    pe.wait_ge(y_added, i * (2 * NY) + (q * NY + b0 + o + 1))
                                for p, (a, b) in enumerate(PRODUCTS):
                                    mm = pe.matmul(y_ps[:, o, 0:TG], vh[:, c, a, m * P:(m + 1) * P],
                                                   wh[:, c, b, g * TG:(g + 1) * TG],
                                                   start=(c == 0 and p == 0), stop=(c == CG - 1 and p == 2))
                                if c == CG - 1:
                                    mm.then_inc(y_ready, 1)
            pe.wait_ge(y_added, N_IT * 2 * NY + 4)
            pe.wait_ge(set_, 1)
            norm.pe(pe)

        def rows_from(n):
            c, g = n // NG, n % NG
            return u[:, g * TG:(g + 1) * TG] if c in EARLY else hid[:, n % 2, :]

        @block.scalar
        def _(act):
            act.sem_inc(gelued, 3)
            act.wait_ge(loaded, 32)
            for k in range(KD):
                act.activation(xh[:, HI, k, :], y[:, k, :], ACT.Copy).then_inc(x_halved, 1)

            with act.Fori(0, N_IT) as i:
                for n in range(NHB):
                    c, g = n // NG, n % NG
                    if c in LIVE:
                        act.wait_ge(h_ready, i * NLB + (LIVE[c] * NG + g + 2))
                        act.wait_ge(w_split, i * NHB + (n + 1))
                        act.activation(hid[:, n % 2, :], h_ps[:, g, 0:TG], ACT.Gelu).then_inc(gelued, 1)
                    elif g == 0:
                        act.wait_ge(y_ready, i * (2 * NY) + (c // CG * NY + 1))
                    act.wait_ge(weighed, i * NHB + (n + 5))
                    act.activation(wh[:, c % CG, HI, g * TG:(g + 1) * TG], rows_from(n),
                                   ACT.Copy).then_inc(w_rounded, 1)
            act.wait_ge(y_added, N_IT * 2 * NY + 4)
            norm.act(act)

        @block.gpsimd
        def _(pool):
            pool.sem_inc(v_split, 2)
            with pool.Fori(0, N_IT) as i:
                for step in SPLITS:
                    c = int(step[1:])
                    if step[0] == "u":
                        pool.wait_ge(u_ready, i * (NC * 16) + (LOADS.index(c) + 1) * 16)
                        pool.wait_ge(h_ready, i * NLB + (max(LIVE[c] - 1, 0) * NG + 1))
                        pool.sem_inc(passed, 1)
                        half, full = uh[:, LIVE[c] % 2], u[:, 0:KD * P]
                        pool.tensor_copy(half[:, HI, :], full).then_inc(u_rounded, 1)
                        pool.wait_ge(u_rounded, i * NL + (LIVE[c] + 1))
                        pool.tensor_tensor(half[:, LO, :], full, half[:, HI, :].bitcast(F32),
                                           ALU.subtract).then_inc(u_split, 1)
                    else:
                        pool.wait_ge(v_ready[c % 2], i * (NC * 8) + (c // 2 + 1) * 16)
                        pool.wait_ge(y_ready, i * (2 * NY) + (c // CG * NY + 1))
                        pool.sem_inc(passed, 1)
                        pool.tensor_copy(vh[:, c % CG, HI, :], v[:, c % 2, :]).then_inc(v_rounded, 1)
                        pool.wait_ge(v_rounded, i * NC + (c + 1))
                        pool.tensor_tensor(vh[:, c % CG, LO, :], v[:, c % 2, :], vh[:, c % CG, HI, :].bitcast(F32),
                                           ALU.subtract).then_inc(v_split, 1)

        @block.vector
        def _(dve):
            dve.memset(ones[:, :], 1.0).then_inc(set_, 1)
            dve.sem_inc(weighed, 4)
            dve.sem_inc(w_split, 2)
            dve.sem_inc(y_added, 4)
            for k in range(KD):
                dve.wait_ge(x_halved, k + 1)
                op = dve.tensor_tensor(xh[:, LO, k, :], y[:, k, :], xh[:, HI, k, :].bitcast(F32), ALU.subtract)
            op.then_inc(x_halved, KD)
            dve.wait_ge(loaded, 48)

            def split(i, n):
                c, cols = n // NG, slice(n % NG * TG, (n % NG + 1) * TG)
                dve.wait_ge(w_rounded, i * NHB + (n + 1))
                dve.tensor_tensor(wh[:, c % CG, LO, cols], rows_from(n), wh[:, c % CG, HI, cols].bitcast(F32),
                                  ALU.subtract).then_inc(w_split, 1)

            with dve.Fori(0, N_IT) as i:
                for q in range(2):
                    for n in range(q * CG * NG, (q + 1) * CG * NG):
                        c, g = n // NG, n % NG
                        if g == 0:
                            dve.wait_ge(g_ready[c % 2], i * (NC * 8) + (c // 2 + 1) * 16)
                        if c in LIVE:
                            dve.wait_ge(gelued, i * NLB + (LIVE[c] * NG + g + 4))
                        elif g == 0:
                            dve.wait_ge(u_ready, i * (NC * 16) + (LOADS.index(c) + 1) * 16)
                        dve.tensor_tensor(rows_from(n), rows_from(n), gate[:, c % 2, g * TG:(g + 1) * TG],
                                          ALU.mult).then_inc(weighed, 1)
                        if n > q * CG * NG:
                            split(i, n - 1)
                    split(i, (q + 1) * CG * NG - 1)
                    for o, (m, g) in enumerate(outs):
                        cols = slice(g * TG, (g + 1) * TG)
                        dve.wait_ge(y_ready, i * (2 * NY) + (q * NY + o + 2))
                        dve.wait_ge(y_added, i * (2 * NY) + (q * NY + 4))
                        dve.tensor_tensor(y[:, m, cols], y_ps[:, o % 4, 0:TG], y[:, m, cols],
                                          ALU.add).then_inc(y_added, 1)
            dve.wait_ge(y_added, N_IT * 2 * NY + 4)
            norm.dve(dve)


def build(nc, dram):
    with ExitStack() as ctx:
        def sem(name):
            return ctx.enter_context(nc.semaphore(name))

        keep = {"con": ctx.enter_context(nc.sbuf_tensor("con", [P, C_W], F32))}
        keep["ident"] = keep["con"][:, C_ID:C_ID + P]
        with nc.sbuf_tensor("routes", [P, 3, NT], F32) as routes:
            keep["routes"] = routes
            with nc.sbuf_tensor("oT", [P, KD, NT], F32) as oT:
                keep["oT"] = oT
                with ExitStack() as mix:
                    for name, shape, dt in (("cs", [P, 2, NT], F32), ("xn", [P, KD, NT], F32),
                                            ("vnat", [P, 10, VW], F32), ("score", [P, SC_W], F32),
                                            ("mbf", [P, MB_W // 2], F32), ("dk", [104, NK], F32),
                                            ("gb", [104, NK], F32), ("ka", [P, NK], F32),
                                            ("causal", [P, P], BF16), ("identb", [P, P], BF16)):
                        keep[name] = mix.enter_context(nc.sbuf_tensor(name, shape, dt))
                    keep["mb"] = keep["mbf"][:, :].bitcast(BF16)
                    mix_inputs(nc, sem, dram, keep)
                    attention_pairs(nc, sem, dram, keep, True)
                    attention_pairs(nc, sem, dram, keep, False)
                with nc.sbuf_tensor("pq", [P, 16, NT], F32) as pq:
                    keep["pq"] = pq
                    with nc.sbuf_tensor("h", [P, KD, NT], F32) as h:
                        keep["h"] = h
                        memory_and_mixer(nc, sem, dram, keep)
                    route(nc, sem, dram, keep)
                spread_gates(nc, sem, dram, keep)
        experts(nc, sem, dram, keep)


OUT = {"o_y": [P, KD, NT], "o_v": [NT, VW], "o_ka": [P, NK], "o_kidx": [HD, NK], "o_fk": [8, HD, NK],
       "o_logf": [8, NK], "o_mk": [P, KD, N_MEM], "o_mv": [P, 2, D]}
SCRATCH = {"s_h": [P, KD, NT], "s_xn": [P, KD, NT], "s_gate": [NKEY, P, NT],
           "s_hid": [N_EARLY, P, NT]}


def constants():
    import numpy as np
    f = np.float32
    con = np.zeros((P, C_W), f)
    con[:, C_ID:C_ID + P] = np.eye(P)
    con[:, C_CAUSAL:C_CAUSAL + P] = np.where(np.arange(P)[None, :] <= np.arange(P)[:, None], 0.0, NEG)
    for m in range(P):
        d = m % HD
        if d < ROT_DIM // 2:
            con[m + ROT_DIM // 2, C_ROT + m] = -1.0
        elif d < ROT_DIM:
            con[m - ROT_DIM // 2, C_ROT + m] = 1.0
    con[:, C_IOTA:C_IOTA + NKEY] = np.arange(NKEY)[None, :]
    for h in range(8):
        con[64 + h, C_SEL + h] = con[96 + h, C_SEL + h] = 1.0
    freq = np.power(f(ROPE_THETA), -np.arange(0, ROT_DIM, 2, dtype=f) / f(ROT_DIM)).astype(f)
    pos = np.concatenate([np.arange(T_P), PAST + np.arange(T_S)]).astype(f)
    ang = (pos[:, None] * freq[None, :]).astype(f)
    cs = np.zeros((P, 2, NT), f)
    cs[:, 0] = 1.0
    for m in range(P):
        if m % HD < ROT_DIM:
            cs[m, 0] = np.cos(ang[:, (m % HD) % (ROT_DIM // 2)])
            cs[m, 1] = np.sin(ang[:, (m % HD) % (ROT_DIM // 2)])
    return con, cs


def kernel(x_prompt, x_sample, cache_dsa_k, cache_dsa_v, cache_dsa_kidx, cache_fox_k, cache_fox_v,
           cache_fox_logf, cache_mem_k, cache_mem_v, mem_prompt, norm_mix_g, w_in, b_fox_f, w_out,
           mem_norm_g, w_mem_kv, norm_mem_g, w_mem_q, w_mem_o, norm_ffn_g, peer_w_q, peer_keys1,
           peer_keys2, peer_u, peer_v, final_norm_g):
    import numpy as np
    import concourse.bacc as bacc
    from concourse.bass_utils import run_bass_kernel_spmd

    def arr(x):
        return np.asarray(x)

    def rows(w):
        return arr(w).reshape(KD, P, -1).transpose(1, 0, 2)

    def blocks(w):
        return arr(w).reshape(KD, P, -1, P).transpose(2, 1, 0, 3)

    def pairs(w):
        return w.reshape(w.shape[0], 2, 4, HD).transpose(0, 2, 1, 3).reshape(w.shape[0], 8 * HD)

    w = arr(w_in)[0]
    aq, ak, av, aqi, aki, aw, fq, fk, fv, ff = np.split(w, np.cumsum(
        [512, 128, 128, 256, 64, 4, 512, 512, 512]), axis=1)
    wo = arr(w_out)[0]
    wo = np.concatenate([pairs(wo[:512].T).T, wo[512:]], axis=0)
    con, cs = constants()
    mkv = arr(w_mem_kv)[0]
    gains = np.stack([arr(mem_norm_g)[0], arr(norm_mem_g)[0], arr(norm_ffn_g)[0]])
    data = {
        "con": con, "cs": cs,
        "xT": rows(np.concatenate([arr(x_prompt)[0], arr(x_sample)[0]]).T),
        "g_mix": arr(norm_mix_g)[0].reshape(KD, P).T, "fb": arr(b_fox_f)[0][:, None],
        "w_rope": np.stack([rows(ak), rows(aqi[:, :P]), rows(aqi[:, P:]), rows(np.concatenate([aki, aki], 1))]),
        "w_f": rows(ff), "w_v": rows(np.concatenate([fv, av, aw], 1)),
        "w_aq": blocks(pairs(aq)), "w_fq": blocks(fq), "w_fk": blocks(fk),
        "c_ka": arr(cache_dsa_k)[0, 0].reshape(PAST, P).T,
        "c_kidx": np.concatenate([arr(cache_dsa_kidx)[0, 0].T] * 2),
        "c_logf": arr(cache_fox_logf)[0, 0].T,
        "c_v": np.concatenate([arr(cache_fox_v)[0, 0].reshape(PAST, 512),
                               arr(cache_dsa_v)[0, 0].reshape(PAST, P)], 1),
        "c_fk": arr(cache_fox_k)[0, 0].reshape(PAST, 512).T.reshape(8, HD, PAST),
        "w_out": blocks(wo), "memT": rows(arr(mem_prompt)[0].T),
        "g_rest": gains.reshape(3, KD, P).transpose(2, 0, 1),
        "w_mk": blocks(mkv[:, :D]), "w_mv": rows(mkv[:, D:]),
        "w_mq": blocks(arr(w_mem_q)[0]), "w_mo": blocks(arr(w_mem_o)[0]), "w_pq": blocks(arr(peer_w_q)[0]),
        "c_mk": rows(arr(cache_mem_k)[0, 0].reshape(N_MEM, D).T),
        "c_mv": arr(cache_mem_v)[0, 0].reshape(2, P, D).transpose(1, 0, 2),
        "keys": np.stack([arr(peer_keys1)[0], arr(peer_keys2)[0]], 1).reshape(16, NKEY, P).transpose(2, 0, 1),
        "ut": arr(peer_u)[0].reshape(NKEY, P, KD, P).transpose(0, 3, 2, 1),
        "v": arr(peer_v)[0].reshape(NKEY, P, D),
        "g_fin": arr(final_norm_g).reshape(KD, P).T,
    }
    data = {k: np.ascontiguousarray(a) for k, a in data.items()}
    nc = bacc.Bacc("TRN2", target_bir_lowering=False, num_devices=1)
    dram = {k: nc.dram_tensor("in_" + k, list(a.shape), F32, kind="ExternalInput").ap() for k, a in data.items()}
    dram |= {k: nc.dram_tensor(k, s, F32, kind="ExternalOutput").ap() for k, s in OUT.items()}
    dram |= {k: nc.dram_tensor(k, s, F32, kind="Internal").ap() for k, s in SCRATCH.items()}
    build(nc, dram)
    r = run_bass_kernel_spmd(nc, [{"in_" + k: a for k, a in data.items()}], core_ids=[0]).results[0]

    y = r["o_y"].transpose(2, 1, 0).reshape(NT, D)
    v, ka, ki, lf = r["o_v"], r["o_ka"].T, r["o_kidx"].T, r["o_logf"].T
    fk = r["o_fk"].transpose(2, 0, 1).reshape(NK, 512)
    mk = r["o_mk"].transpose(2, 1, 0)
    mv = r["o_mv"].transpose(1, 0, 2)
    p, s, n = slice(0, T_P), slice(T_P + PAST, NK), slice(T_P, NT)

    def state(k, t):
        m = v[t].shape[0]
        return (ka[k].reshape(1, 1, m, 2, HD), v[t, 512:].reshape(1, 1, m, 2, HD), ki[k].reshape(1, 1, m, HD),
                fk[k].reshape(1, 1, m, 8, HD), v[t, :512].reshape(1, 1, m, 8, HD), lf[k].reshape(1, 1, m, 8))

    return (y[None, :T_P], y[None, T_P:]) + state(p, p) + (
        mk.reshape(1, 1, N_MEM, MH, MHD), mv.reshape(1, 1, N_MEM, MH, MHD)) + state(s, n)
```
